# Optimizing a Trainium2 kernel written in Bass

```python
import jax, jax.numpy as jnp
from jax import lax
import numpy as np

D_MODEL = 1024
BATCH = 1
SEQ = 128
DEPTH = 2
DEC_BATCH = 1
DEC_SEQ = 512
PAST_LEN = 128

GRID_W = 64
EPS = 1e-6
GLA_HEADS = 4
GLA_DK = 64
GLA_DV = 128
GLA_LOWRANK = 16
GLA_TAU = 16.0
GLA_CHUNK = 64
GLA_QK = GLA_HEADS * GLA_DK
GLA_V = GLA_HEADS * GLA_DV
POOL_GROUPS = 4
POOL_GROUP_DIM = 128
POOL_WINDOWS = (2, 4, 8, 16)
POOL_DIM = POOL_GROUPS * POOL_GROUP_DIM
IN0_DIM = 2 * GLA_QK + 2 * GLA_V + 2 * GLA_LOWRANK + POOL_DIM
MIX0_DIM = GLA_V + POOL_DIM
ATT_HEADS = 16
ATT_KV_HEADS = 4
ATT_HD = 64
ATT_WINDOW = 128
ATT_BLOCK = 128
ROPE_THETA = 10000.0
IN1_DIM = (ATT_HEADS + 2 * ATT_KV_HEADS) * ATT_HD
PEER_HEADS = 8
PEER_NKEYS = 128
PEER_N = PEER_NKEYS * PEER_NKEYS
PEER_QDIM = 256
PEER_HALF = PEER_QDIM // 2
PEER_TOPK = 16
PEER_TOK_BLOCK = 128

kernel_name = 'hybrid_flow_ctx_prefix_step'

def rms_norm(x, gain):
    xf = x.astype(jnp.float32)
    y = xf * lax.rsqrt(jnp.mean(xf * xf, axis=-1, keepdims=True) + EPS)
    return (y * gain.astype(jnp.float32)).astype(x.dtype)

def split_cols(t, sizes):
    return jnp.split(t, np.cumsum(sizes)[:-1].tolist(), axis=-1)

def modulation(cond, w_mod, b_mod):
    m = jax.nn.silu(cond) @ w_mod + b_mod
    return jnp.split(m[:, None, :], 6, axis=-1)

def modulate(x, gain, shift, scale):
    return rms_norm(x, gain) * (1.0 + scale) + shift

def gla_chunked(q, k, v, log_a, s0):
    B, S, H, DK = q.shape
    DV = v.shape[-1]
    C = GLA_CHUNK
    n = S // C

    def blocks(t):
        return t.astype(jnp.float32).reshape(B, n, C, H, t.shape[-1]).transpose(1, 0, 3, 2, 4)

    qc, kc, vc, ac = blocks(q), blocks(k), blocks(v), blocks(log_a)
    b = jnp.cumsum(ac, axis=3)
    b_tot = b[:, :, :, -1, :]
    causal = jnp.tril(jnp.ones((C, C), dtype=bool))
    diff = b[:, :, :, :, None, :] - b[:, :, :, None, :, :]
    decay = jnp.exp(jnp.where(causal[:, :, None], diff, -jnp.inf))
    scores = jnp.einsum('nbhtd,nbhsd,nbhtsd->nbhts', qc, kc, decay)
    o_intra = jnp.einsum('nbhts,nbhsv->nbhtv', scores, vc)
    q_in = qc * jnp.exp(b)
    k_up = kc * jnp.exp(b_tot[:, :, :, None, :] - b)

    def step(state, xs):
        qi, ki, vi, bt = xs
        o = jnp.einsum('bhtd,bhdv->bhtv', qi, state)
        state = state * jnp.exp(bt)[..., None] + jnp.einsum('bhsd,bhsv->bhdv', ki, vi)
        return state, o

    s_fin, o_inter = lax.scan(step, s0.astype(jnp.float32), (q_in, k_up, vc, b_tot))
    o = (o_intra + o_inter).transpose(1, 0, 3, 2, 4).reshape(B, S, H, DV)
    return o, s_fin

def pool_mixer(p, pool_w, pool_scale):
    B, S, _ = p.shape
    pf = p.astype(jnp.float32)
    cs = jnp.concatenate([jnp.zeros((B, 1, POOL_DIM), jnp.float32), jnp.cumsum(pf, axis=1)], axis=1)
    pos = jnp.arange(S)
    diffs = []
    for gi, w in enumerate(POOL_WINDOWS):
        lo = jnp.clip(pos - w // 2, 0, S)
        hi = jnp.clip(pos + w // 2, 0, S)
        sl = slice(gi * POOL_GROUP_DIM, (gi + 1) * POOL_GROUP_DIM)
        cg = cs[:, :, sl]
        mean = (cg[:, hi] - cg[:, lo]) / (hi - lo).astype(jnp.float32)[None, :, None]
        diffs.append(mean - pf[:, :, sl])
    d = jnp.stack(diffs, axis=2)
    y = jnp.einsum('bsgi,gio->bsgo', d, pool_w.astype(jnp.float32)).reshape(B, S, POOL_DIM)
    return (y * pool_scale.astype(jnp.float32)).astype(p.dtype)

def mixer_ab(h, w_in, w_af, b_af, w_ab, b_ab, gla_norm, pool_w, pool_scale, w_out, s0_f, s0_b):
    B, S, _ = h.shape
    q, k, v, r, za_f, za_b, pin = split_cols(
        h @ w_in, (GLA_QK, GLA_QK, GLA_V, GLA_V, GLA_LOWRANK, GLA_LOWRANK, POOL_DIM))
    q = q.reshape(B, S, GLA_HEADS, GLA_DK) * (GLA_DK ** -0.5)
    k = k.reshape(B, S, GLA_HEADS, GLA_DK)
    v = v.reshape(B, S, GLA_HEADS, GLA_DV)
    la_f = (jax.nn.log_sigmoid((za_f @ w_af + b_af).astype(jnp.float32)) / GLA_TAU).reshape(B, S, GLA_HEADS, GLA_DK)
    la_b = (jax.nn.log_sigmoid((za_b @ w_ab + b_ab).astype(jnp.float32)) / GLA_TAU).reshape(B, S, GLA_HEADS, GLA_DK)
    o_f, s_f = gla_chunked(q, k, v, la_f, s0_f)
    o_b, s_b = gla_chunked(q[:, ::-1], k[:, ::-1], v[:, ::-1], la_b[:, ::-1], s0_b)
    o = rms_norm(o_f + o_b[:, ::-1], gla_norm).astype(h.dtype)
    gla_out = (o * jax.nn.silu(r.reshape(B, S, GLA_HEADS, GLA_DV))).reshape(B, S, GLA_V)
    pool_out = pool_mixer(pin, pool_w, pool_scale)
    y = jnp.concatenate([gla_out, pool_out], axis=-1) @ w_out
    return y, s_f, s_b

def attn_qkv(h, w_in, q_gain, k_gain):
    B, S, _ = h.shape
    q, k, v = split_cols(h @ w_in, (ATT_HEADS * ATT_HD, ATT_KV_HEADS * ATT_HD, ATT_KV_HEADS * ATT_HD))
    q = rms_norm(q.reshape(B, S, ATT_HEADS, ATT_HD), q_gain)
    k = rms_norm(k.reshape(B, S, ATT_KV_HEADS, ATT_HD), k_gain)
    v = v.reshape(B, S, ATT_KV_HEADS, ATT_HD)
    return q, k, v

def axial_rope(x):
    S = x.shape[1]
    rows = S // GRID_W
    row = jnp.repeat(jnp.arange(rows), GRID_W)
    col = jnp.tile(jnp.arange(GRID_W), rows)
    half = ATT_HD // 2
    inv_freq = 1.0 / (ROPE_THETA ** (jnp.arange(0, half, 2, dtype=jnp.float32) / half))
    xf = x.astype(jnp.float32)

    def rot(xa, pos):
        ang = pos.astype(jnp.float32)[:, None] * inv_freq[None, :]
        cos = jnp.cos(ang)[None, :, None, :]
        sin = jnp.sin(ang)[None, :, None, :]
        x1, x2 = xa[..., :half // 2], xa[..., half // 2:]
        return jnp.concatenate([x1 * cos - x2 * sin, x2 * cos + x1 * sin], axis=-1)

    return jnp.concatenate([rot(xf[..., :half], row), rot(xf[..., half:], col)], axis=-1).astype(x.dtype)

def context_attention(q, k, v, sink):
    B, L, H, HD = q.shape
    KV = k.shape[2]
    G = H // KV
    qg = q.reshape(B, L, KV, G, HD) * (HD ** -0.5)
    s = jnp.einsum('bqkgd,blkd->bkgql', qg, k).astype(jnp.float32)
    sk = jnp.broadcast_to(sink.astype(jnp.float32).reshape(KV, G)[None, :, :, None, None], s.shape[:-1] + (1,))
    probs = jax.nn.softmax(jnp.concatenate([s, sk], axis=-1), axis=-1)
    o = jnp.einsum('bkgql,blkd->bqkgd', probs[..., :L].astype(v.dtype), v)
    return o.reshape(B, L, H * HD)

def window_attention(q, k, v, k_ctx, v_ctx, sink):
    B, S, H, HD = q.shape
    KV = k.shape[2]
    G = H // KV
    W = ATT_BLOCK
    nb = S // W
    L = k_ctx.shape[1]
    qb = q.reshape(B, nb, W, KV, G, HD) * (HD ** -0.5)
    pad = ((0, 0), (W, W), (0, 0), (0, 0))
    kp = jnp.pad(k, pad).reshape(B, nb + 2, W, KV, HD)
    vp = jnp.pad(v, pad).reshape(B, nb + 2, W, KV, HD)
    kb = jnp.concatenate([kp[:, :-2], kp[:, 1:-1], kp[:, 2:]], axis=2)
    vb = jnp.concatenate([vp[:, :-2], vp[:, 1:-1], vp[:, 2:]], axis=2)
    s_loc = jnp.einsum('bnqkgd,bnjkd->bnkgqj', qb, kb).astype(jnp.float32)
    qpos = jnp.arange(S).reshape(nb, W)
    kpos = (jnp.arange(nb)[:, None] - 1) * W + jnp.arange(3 * W)[None, :]
    valid = ((kpos[:, None, :] >= 0) & (kpos[:, None, :] < S)
             & (jnp.abs(qpos[:, :, None] - kpos[:, None, :]) <= ATT_WINDOW))
    s_loc = jnp.where(valid[None, :, None, None], s_loc, -jnp.inf)
    s_ctx = jnp.einsum('bnqkgd,blkd->bnkgql', qb, k_ctx.astype(q.dtype)).astype(jnp.float32)
    sk = jnp.broadcast_to(sink.astype(jnp.float32).reshape(KV, G)[None, None, :, :, None, None],
                          s_loc.shape[:-1] + (1,))
    probs = jax.nn.softmax(jnp.concatenate([s_loc, s_ctx, sk], axis=-1), axis=-1)
    p_loc = probs[..., :3 * W].astype(v.dtype)
    p_ctx = probs[..., 3 * W:3 * W + L].astype(v.dtype)
    o = (jnp.einsum('bnkgqj,bnjkd->bnqkgd', p_loc, vb)
         + jnp.einsum('bnkgql,blkd->bnqkgd', p_ctx, v_ctx.astype(v.dtype)))
    return o.reshape(B, S, H * HD)

def peer(h, w_q, keys, u, v):
    B, S, D = h.shape
    T = B * S
    x = h.reshape(T, D)
    qh = (x @ w_q).reshape(T, PEER_HEADS, 2, PEER_HALF)
    s = jnp.einsum('thcd,hcnd->thcn', qh, keys).astype(jnp.float32)
    s1, i1 = lax.top_k(s[:, :, 0], PEER_TOPK)
    s2, i2 = lax.top_k(s[:, :, 1], PEER_TOPK)
    cand = (s1[..., :, None] + s2[..., None, :]).reshape(T, PEER_HEADS, PEER_TOPK * PEER_TOPK)
    cidx = (i1[..., :, None] * PEER_NKEYS + i2[..., None, :]).reshape(T, PEER_HEADS, PEER_TOPK * PEER_TOPK)
    top_s, top_pos = lax.top_k(cand, PEER_TOPK)
    experts = jnp.take_along_axis(cidx, top_pos, axis=-1)
    gates = jax.nn.softmax(top_s, axis=-1)
    nblk = T // PEER_TOK_BLOCK

    def block(args):
        xb, eb, gb = args
        act = jax.nn.gelu(jnp.einsum('thkd,td->thk', u[eb], xb))
        return jnp.einsum('thk,thkd->td', (gb * act).astype(xb.dtype), v[eb])

    y = lax.map(block, (x.reshape(nblk, PEER_TOK_BLOCK, D),
                        experts.reshape(nblk, PEER_TOK_BLOCK, PEER_HEADS, PEER_TOPK),
                        gates.reshape(nblk, PEER_TOK_BLOCK, PEER_HEADS, PEER_TOPK)))
    return y.reshape(B, S, D)

def setup_inputs(seed: int = 0) -> dict:
    key = jax.random.key(seed)
    ks = iter(jax.random.split(key, 64))

    def nrm(shape, scale=1.0):
        return jax.random.normal(next(ks), shape, jnp.float32) * scale

    D = D_MODEL
    inp = {}
    inp['x_prompt'] = nrm((BATCH, SEQ, D))
    inp['x_sample'] = nrm((DEC_BATCH, DEC_SEQ, D))
    inp['state_l0_gla'] = nrm((DEC_BATCH, 2, GLA_HEADS, GLA_DK, GLA_DV))
    inp['cache_l1_k'] = nrm((DEC_BATCH, PAST_LEN, ATT_KV_HEADS, ATT_HD))
    inp['cache_l1_v'] = nrm((DEC_BATCH, PAST_LEN, ATT_KV_HEADS, ATT_HD))
    inp['c'] = nrm((DEC_BATCH, D))
    inp['c_ctx'] = nrm((D,))
    inp['l0_w_mod'] = nrm((D, 6 * D), 0.5 * D ** -0.5)
    inp['l0_b_mod'] = nrm((6 * D,), 0.05)
    inp['l0_norm1'] = 1.0 + nrm((D,), 0.05)
    inp['l0_w_in'] = nrm((D, IN0_DIM), D ** -0.5)
    inp['l0_w_alpha_f'] = nrm((GLA_LOWRANK, GLA_QK), GLA_LOWRANK ** -0.5)
    inp['l0_b_alpha_f'] = 2.0 + nrm((GLA_QK,), 0.5)
    inp['l0_w_alpha_b'] = nrm((GLA_LOWRANK, GLA_QK), GLA_LOWRANK ** -0.5)
    inp['l0_b_alpha_b'] = 2.0 + nrm((GLA_QK,), 0.5)
    inp['l0_gla_norm'] = 1.0 + nrm((GLA_DV,), 0.05)
    inp['l0_pool_w'] = nrm((POOL_GROUPS, POOL_GROUP_DIM, POOL_GROUP_DIM), POOL_GROUP_DIM ** -0.5)
    inp['l0_pool_scale'] = 0.5 + nrm((POOL_DIM,), 0.1)
    inp['l0_w_out'] = nrm((MIX0_DIM, D), MIX0_DIM ** -0.5)
    inp['l0_norm2'] = 1.0 + nrm((D,), 0.05)
    inp['l0_peer_wq'] = nrm((D, PEER_HEADS * PEER_QDIM), D ** -0.5)
    inp['l0_peer_keys'] = nrm((PEER_HEADS, 2, PEER_NKEYS, PEER_HALF), PEER_HALF ** -0.5)
    inp['l0_peer_u'] = nrm((PEER_N, D), D ** -0.5)
    inp['l0_peer_v'] = nrm((PEER_N, D), 0.5)
    inp['l1_w_mod'] = nrm((D, 6 * D), 0.5 * D ** -0.5)
    inp['l1_b_mod'] = nrm((6 * D,), 0.05)
    inp['l1_norm1'] = 1.0 + nrm((D,), 0.05)
    inp['l1_w_in'] = nrm((D, IN1_DIM), D ** -0.5)
    inp['l1_q_norm'] = 1.0 + nrm((ATT_HD,), 0.05)
    inp['l1_k_norm'] = 1.0 + nrm((ATT_HD,), 0.05)
    inp['l1_sink'] = nrm((ATT_HEADS,), 0.5)
    inp['l1_w_out'] = nrm((ATT_HEADS * ATT_HD, D), (ATT_HEADS * ATT_HD) ** -0.5)
    inp['l1_norm2'] = 1.0 + nrm((D,), 0.05)
    inp['l1_peer_wq'] = nrm((D, PEER_HEADS * PEER_QDIM), D ** -0.5)
    inp['l1_peer_keys'] = nrm((PEER_HEADS, 2, PEER_NKEYS, PEER_HALF), PEER_HALF ** -0.5)
    inp['l1_peer_u'] = nrm((PEER_N, D), D ** -0.5)
    inp['l1_peer_v'] = nrm((PEER_N, D), 0.5)
    return inp

def reference(x_prompt, x_sample, state_l0_gla, cache_l1_k, cache_l1_v, c, c_ctx,
              l0_w_mod, l0_b_mod, l0_norm1, l0_w_in, l0_w_alpha_f, l0_b_alpha_f, l0_w_alpha_b, l0_b_alpha_b,
              l0_gla_norm, l0_pool_w, l0_pool_scale, l0_w_out, l0_norm2, l0_peer_wq, l0_peer_keys, l0_peer_u, l0_peer_v,
              l1_w_mod, l1_b_mod, l1_norm1, l1_w_in, l1_q_norm, l1_k_norm, l1_sink, l1_w_out,
              l1_norm2, l1_peer_wq, l1_peer_keys, l1_peer_u, l1_peer_v):
    layer_mod = ((l0_w_mod, l0_b_mod, l0_norm1), (l1_w_mod, l1_b_mod, l1_norm1))
    layer_peer = ((l0_norm2, l0_peer_wq, l0_peer_keys, l0_peer_u, l0_peer_v),
                  (l1_norm2, l1_peer_wq, l1_peer_keys, l1_peer_u, l1_peer_v))
    mix_ab = (l0_w_in, l0_w_alpha_f, l0_b_alpha_f, l0_w_alpha_b, l0_b_alpha_b,
              l0_gla_norm, l0_pool_w, l0_pool_scale, l0_w_out)

    cond_ctx = c_ctx[None, :]
    xp = x_prompt
    bp = x_prompt.shape[0]
    for li in range(DEPTH):
        w_mod, b_mod, n1 = layer_mod[li]
        sh1, sc1, g1, sh2, sc2, g2 = modulation(cond_ctx, w_mod, b_mod)
        h = modulate(xp, n1, sh1, sc1)
        if li % 2 == 0:
            s0 = jnp.zeros((bp, GLA_HEADS, GLA_DK, GLA_DV), jnp.float32)
            out, s_f, s_b = mixer_ab(h, *mix_ab, s0, s0)
            new_state_l0_gla = jnp.stack([s_f, s_b], axis=1).astype(x_prompt.dtype)
        else:
            q, k, v = attn_qkv(h, l1_w_in, l1_q_norm, l1_k_norm)
            out = context_attention(q, k, v, l1_sink) @ l1_w_out
            new_cache_l1_k = k
            new_cache_l1_v = v
        xp = xp + g1 * out
        n2, wq, pkeys, pu, pv = layer_peer[li]
        xp = xp + g2 * peer(modulate(xp, n2, sh2, sc2), wq, pkeys, pu, pv)
    y_prompt = xp

    xs = x_sample
    for li in range(DEPTH):
        w_mod, b_mod, n1 = layer_mod[li]
        sh1, sc1, g1, sh2, sc2, g2 = modulation(c, w_mod, b_mod)
        h = modulate(xs, n1, sh1, sc1)
        if li % 2 == 0:
            out, _, _ = mixer_ab(h, *mix_ab, state_l0_gla[:, 0], state_l0_gla[:, 1])
        else:
            q, k, v = attn_qkv(h, l1_w_in, l1_q_norm, l1_k_norm)
            q = axial_rope(q)
            k = axial_rope(k)
            out = window_attention(q, k, v, cache_l1_k, cache_l1_v, l1_sink) @ l1_w_out
        xs = xs + g1 * out
        n2, wq, pkeys, pu, pv = layer_peer[li]
        xs = xs + g2 * peer(modulate(xs, n2, sh2, sc2), wq, pkeys, pu, pv)
    y_sample = xs

    return (y_prompt, y_sample, new_state_l0_gla, new_cache_l1_k, new_cache_l1_v)


_drawn_inputs = setup_inputs


def setup_inputs(seed=0):
    import zlib

    import numpy as np

    out = dict(_drawn_inputs(seed))
    spreads = {}
    factors = {'state_l0_gla': 6.123,
     'cache_l1_k': 3.411,
     'cache_l1_v': 2.876,
     'l0_gla_norm': 4.029,
     'l1_q_norm': 8.0,
     'l1_sink': 64.0,
     'l1_norm2': 2.87}
    for name, (base, spread) in spreads.items():
        noise = np.random.default_rng([zlib.crc32(name.encode()), seed]).standard_normal(out[name].shape)
        drawn = base * np.exp(spread * noise) if base else spread * noise
        out[name] = __import__('jax').numpy.asarray(drawn.astype(out[name].dtype))
    for name, factor in factors.items():
        out[name] = (out[name] * factor).astype(out[name].dtype)
    return out
```

```python
from contextlib import ExitStack

import numpy as np

import concourse.bass as bass
from concourse import mybir

F32 = mybir.dt.float32
I32 = mybir.dt.int32
U32 = mybir.dt.uint32
ALU = mybir.AluOpType
ACT = mybir.ActivationFunctionType
AX = mybir.AxisListType

P = 128
D = 1024
DK = D // P
PROMPT_TILES = 1
LATENT_TILES = 4
TILES = PROMPT_TILES + LATENT_TILES
TOK = TILES * P
EPS = 1e-6
HEADS0, DKH, DV = 4, 64, 128
QK = HEADS0 * DKH
VW = HEADS0 * DV
LOWRANK = 16
POOL_WINDOWS = (2, 4, 8, 16)
IN0 = 2 * QK + 2 * VW + 2 * LOWRANK + VW
Q0, K0, V0, R0, Z0, PIN0 = 0, QK, 2 * QK, 2 * QK + VW, 2 * QK + 2 * VW, 2 * QK + 2 * VW + 2 * LOWRANK
LEVELS = 7
QH, KVH, HD = 16, 4, 64
IN1 = (QH + 2 * KVH) * HD
GRID_W = 64
PH, NKEYS, TOPK = 8, 128, 16
SLOTS = PH * TOPK
RING = 8
MODW = 6 * D


def decay_constants():
    u = np.arange(P)[:, None]
    x = np.arange(P)[None, :]
    sums = np.zeros((2, LEVELS + 1, P, P), np.float32)
    masks = np.zeros((2, LEVELS, P, P), np.int32)
    for lv in range(LEVELS):
        m = P >> (lv + 1)
        mid = x // (2 * m) * 2 * m + m
        upper = (x // m) % 2 == 1
        sums[0, lv] = np.where(upper, (u >= mid) & (u <= x), (u > x) & (u < mid))
        sums[1, lv] = np.where(upper, (u >= mid) & (u < x), (u >= x) & (u < mid))
        s, t = u, x
        same = s // (2 * m) == t // (2 * m)
        masks[0, lv] = same & ((s // m) % 2 == 0) & ((t // m) % 2 == 1)
        masks[1, lv] = same & ((s // m) % 2 == 1) & ((t // m) % 2 == 0)
    sums[0, LEVELS] = u <= x
    sums[1, LEVELS] = u >= x
    key = np.stack([(u > x), (u < x)]).astype(np.float32)
    scale = np.float32(1 / 16)
    return (np.ascontiguousarray(sums.transpose(2, 0, 1, 3)) * scale,
            np.ascontiguousarray(key.transpose(1, 0, 2)) * scale,
            np.ascontiguousarray(masks.transpose(2, 0, 1, 3)))


def pool_constants():
    out = np.zeros((6, len(POOL_WINDOWS), P, P), np.float32)
    tok = np.arange(P)
    for v, (first, last) in enumerate(((1, 1), (1, 0), (0, 0), (0, 1))):
        for g, w in enumerate(POOL_WINDOWS):
            lo, hi = tok - w // 2, tok + w // 2
            if first:
                lo = np.maximum(lo, 0)
            if last:
                hi = np.minimum(hi, P)
            n = (hi - lo).astype(np.float32)
            src = np.arange(P)[:, None]
            out[v, g] = ((src >= lo) & (src < hi)) / n - (src == tok)
    for g, w in enumerate(POOL_WINDOWS):
        src = np.arange(P)[:, None]
        out[4, g] = (src - P >= tok - w // 2) / np.float32(w)
        out[5, g] = (src + P < tok + w // 2) / np.float32(w)
    return np.ascontiguousarray(out.transpose(2, 0, 1, 3))


def rope_constants():
    half = HD // 2
    inv = (1.0 / (np.float32(10000.0) ** (np.arange(0, half, 2, dtype=np.float32) / half))).astype(np.float32)
    pos = np.arange(LATENT_TILES * P)
    cos, sin = [], []
    for p in (pos // GRID_W, pos % GRID_W):
        ang = p.astype(np.float32)[:, None] * inv[None, :]
        cos += [np.cos(ang), np.cos(ang)]
        sin += [-np.sin(ang), np.sin(ang)]
    shape = (LATENT_TILES, P, HD)
    return np.ascontiguousarray(np.stack([np.concatenate(cos, -1).reshape(shape), np.concatenate(sin, -1).reshape(shape)])
                                .astype(np.float32).transpose(2, 0, 1, 3))


def window_constants():
    q, k = np.arange(P)[:, None], np.arange(P)[None, :]
    out = np.zeros((P, 3, P), np.float32)
    out[:, 0] = np.where(k >= q, 0, -1e30)
    out[:, 2] = np.where(k <= q, 0, -1e30)
    return out


class Stage:

    def __init__(self, nc, tag):
        self.nc, self.tag, self.stack, self.sems = nc, tag, ExitStack(), []

    def __enter__(self):
        self.stack.__enter__()
        return self

    def __exit__(self, *e):
        done = self.stack.__exit__(*e)
        if self.sems:
            self.nc.clear_and_free_semaphores(self.sems)
            self.nc.all_engine_barrier()
        return done

    def sb(self, name, shape, dt=F32):
        return self.stack.enter_context(self.nc.sbuf_tensor(f"{self.tag}_{name}", shape, dt))

    def ps(self, name, shape):
        return self.stack.enter_context(self.nc.psum_tensor(f"{self.tag}_{name}", shape, F32))

    def sem(self, name):
        self.sems.append(self.nc.alloc_semaphore(f"{self.tag}_{name}"))
        return self.sems[-1]


class Order:

    def __init__(self, eng, sem):
        self.eng, self.sem, self.n = eng, sem, 0

    def __call__(self, ins):
        ins.then_inc(self.sem, 1)
        self.n += 1
        self.eng.wait_ge(self.sem, self.n)


def broadcast_row(row):
    return row.partition_broadcast(P)


def modulation_stage(nc, a, mods):
    CH, WSLOTS = 512, 4
    per_layer = MODW // CH
    with Stage(nc, "mod") as s:
        w = s.sb("w", [P, WSLOTS, DK, CH])
        cond = s.sb("cond", [P, DK, 2])
        gate = s.sb("gate", [P, DK, 2])
        act_c = s.sb("silu", [P, DK, 2])
        m = s.sb("m", [2, 2 * MODW])
        ps = s.ps("ps", [P, 2, CH])
        cond_in, bias_in = s.sem("cond_in"), s.sem("bias_in")
        w_in = [s.sem(f"w_in{i}") for i in range(WSLOTS)]
        exp_done, dve_order, silu_done = s.sem("exp_done"), s.sem("dve_order"), s.sem("silu_done")
        w_free, mm_done, add_done, stored = s.sem("w_free"), s.sem("mm_done"), s.sem("add_done"), s.sem("stored")
        block = s.stack.enter_context(nc.Block())

        @block.sync
        def _(sp):
            with nc.allow_non_contiguous_dma(reason="two vectors laid onto partitions"):
                sp.dma_start(cond[:, :, 0], a["c_ctx"].rearrange("(k p) -> p k", p=P)).then_inc(cond_in, 16)
                sp.dma_start(cond[:, :, 1], a["c"].rearrange("o (k p) -> p (o k)", p=P)).then_inc(cond_in, 16)
            for layer in range(2):
                sp.dma_start(m[:, layer * MODW:(layer + 1) * MODW],
                             a[f"l{layer}_b_mod"].partition_broadcast(2)).then_inc(bias_in, 16)
            for layer in range(2):
                wv = a[f"l{layer}_w_mod"].rearrange("(k p) n -> p k n", p=P)
                with sp.Fori(0, per_layer // WSLOTS) as i:
                    for slot in range(WSLOTS):
                        n = layer * per_layer + i * WSLOTS + slot
                        sp.wait_ge(w_free, n + 1)
                        sp.dma_start(w[:, slot], wv[:, :, bass.ds((i * WSLOTS + slot) * CH, CH)]).then_inc(w_in[slot], 16)
            sp.wait_ge(add_done, 2 * per_layer)
            sp.dma_start(mods, m[:, :]).then_inc(stored, 16)
            sp.wait_ge(stored, 16)

        @block.scalar
        def _(act):
            act.wait_ge(cond_in, 32)
            nc.scalar.activation(gate[:], cond[:], ACT.Exp, scale=-1.0).then_inc(exp_done, 1)

        @block.vector
        def _(dve):
            order = Order(dve, dve_order)
            dve.wait_ge(exp_done, 1)
            order(nc.vector.tensor_scalar_add(gate[:], gate[:], 1.0))
            order(nc.vector.reciprocal(gate[:], gate[:]))
            nc.vector.tensor_tensor(act_c[:], cond[:], gate[:], ALU.mult).then_inc(silu_done, 1)
            dve.wait_ge(bias_in, 32)
            with dve.Fori(0, per_layer) as i:
                for b in range(2):
                    dve.wait_ge(mm_done, 2 * i + b + 1)
                    mc = m[:, bass.ds((2 * i + b) * CH, CH)]
                    nc.vector.tensor_tensor(mc, mc, ps[0:2, b, :], ALU.add).then_inc(add_done, 1)

        def mod_chunk(pe, slot, n, rnd, first):
            pe.wait_ge(w_in[slot], rnd * 16 + 16)
            if not first or slot >= 2:
                pe.wait_ge(add_done, n - 1)
            for k in range(DK):
                mm = nc.tensor.matmul(ps[0:2, slot % 2, :], act_c[:, k, :], w[:, slot, k, :],
                                      start=(k == 0), stop=(k == DK - 1))
            mm.then_inc(mm_done, 1)
            pe.wait_ge(mm_done, n + 1)
            pe.sem_inc(w_free, 1)

        @block.tensor
        def _(pe):
            pe.sem_inc(w_free, WSLOTS)
            pe.wait_ge(silu_done, 1)
            for slot in range(WSLOTS):
                mod_chunk(pe, slot, slot, 0, first=True)
            with pe.Fori(1, 2 * per_layer // WSLOTS) as i:
                for slot in range(WSLOTS):
                    mod_chunk(pe, slot, i * WSLOTS + slot, i, first=False)


def load_stage(nc, a, env):
    with Stage(nc, "load") as s:
        loaded = s.sem("loaded")
        block = s.stack.enter_context(nc.Block())

        @block.sync
        def _(sp):
            sp.dma_start(env["x"][:, 0, :], a["x_prompt"].rearrange("o p d -> p (o d)")).then_inc(loaded, 16)
            sp.dma_start(env["x"][:, 1:TILES, :], a["x_sample"].rearrange("o (t p) d -> p (o t) d", p=P)).then_inc(loaded, 16)
            sp.dma_start(env["ident"][:], a["k_ident"]).then_inc(loaded, 16)
            sp.wait_ge(loaded, 48)


def norm_stage(nc, a, env, tag, layer, norm, which, hT):
    x, h, ident = env["x"], env["h"], env["ident"]
    base = layer * MODW + which * 3 * D
    with Stage(nc, tag) as s:
        gain = s.sb("gain", [P, D])
        ma = s.sb("scale", [P, 2, D])
        mb = s.sb("shift", [P, 2, D])
        junk = s.sb("junk", [P, D])
        ss = s.sb("ss", [P, TILES])
        ps = s.ps("ps", [P, 2, D])
        mod_in, sq_done, mean_done, sqrt_done = s.sem("mod_in"), s.sem("sq_done"), s.sem("mean_done"), s.sem("sqrt_done")
        dve_order, act_order, h_done, tr_done, hT_done = (s.sem("dve_order"), s.sem("act_order"), s.sem("h_done"),
                                                          s.sem("tr_done"), s.sem("hT_done"))
        block = s.stack.enter_context(nc.Block())

        @block.sync
        def _(sp):
            sp.dma_start(gain[:], broadcast_row(norm)).then_inc(mod_in, 16)
            for c in range(2):
                sp.dma_start(ma[:, c, :], broadcast_row(env["mods"][c, base + D:base + 2 * D])).then_inc(mod_in, 16)
                sp.dma_start(mb[:, c, :], broadcast_row(env["mods"][c, base:base + D])).then_inc(mod_in, 16)

        @block.scalar
        def _(act):
            order = Order(act, act_order)
            for t in range(TILES):
                i = nc.scalar.activation(junk[:], x[:, t, :], ACT.Square, accum_out=ss[:, t:t + 1])
                if t < TILES - 1:
                    order(i)
            i.then_inc(sq_done, 1)
            act.wait_ge(mean_done, 1)
            nc.scalar.activation(ss[:], ss[:], ACT.Sqrt).then_inc(sqrt_done, 1)
            for t in range(TILES):
                act.wait_ge(tr_done, t + 1)
                nc.scalar.activation(hT[:, :, t * P:(t + 1) * P],
                                     ps[:, t % 2, :].rearrange("p (k n) -> p k n", k=DK), ACT.Copy).then_inc(hT_done, 1)

        @block.vector
        def _(dve):
            order = Order(dve, dve_order)
            dve.wait_ge(mod_in, 80)
            for c in range(2):
                order(nc.vector.scalar_tensor_tensor(ma[:, c, :], ma[:, c, :], 1.0, gain[:], ALU.add, ALU.mult))
            dve.wait_ge(sq_done, 1)
            nc.vector.tensor_scalar(ss[:], ss[:], 1.0 / D, EPS, ALU.mult, ALU.add).then_inc(mean_done, 1)
            dve.wait_ge(sqrt_done, 1)
            order(nc.vector.reciprocal(ss[:], ss[:]))
            for t in range(TILES):
                c = 0 if t < PROMPT_TILES else 1
                order(nc.vector.scalar_tensor_tensor(h[:, t, :], x[:, t, :], ss[:, t:t + 1], ma[:, c, :], ALU.mult, ALU.mult))
                nc.vector.tensor_tensor(h[:, t, :], h[:, t, :], mb[:, c, :], ALU.add).then_inc(h_done, 1)

        @block.tensor
        def _(pe):
            for t in range(TILES):
                pe.wait_ge(h_done, t + 1)
                if t >= 2:
                    pe.wait_ge(hT_done, t - 1)
                for k in range(DK):
                    mm = nc.tensor.transpose(ps[:, t % 2, k * P:(k + 1) * P], h[:, t, k * P:(k + 1) * P], ident[:])
                mm.then_inc(tr_done, 1)


def projection_stage(nc, tag, hT, w_dram, n_out, chunk, out):
    n_chunks = n_out // chunk
    with Stage(nc, tag) as s:
        w = s.sb("w", [P, 2, DK, chunk])
        ps = s.ps("ps", [P, 4, 512])
        w_in = [s.sem(f"w_in{i}") for i in range(2)]
        mm_done, out_done = s.sem("mm_done"), s.sem("out_done")
        block = s.stack.enter_context(nc.Block())
        wv = w_dram.rearrange("(k p) n -> p k n", p=P)

        @block.sync
        def _(sp):
            for n in range(n_chunks):
                if n >= 2:
                    sp.wait_ge(mm_done, (n - 1) * TILES)
                sp.dma_start(w[:, n % 2], wv[:, :, n * chunk:(n + 1) * chunk]).then_inc(w_in[n % 2], 16)

        @block.tensor
        def _(pe):
            for n in range(n_chunks):
                pe.wait_ge(w_in[n % 2], n // 2 * 16 + 16)
                for t in range(TILES):
                    i = n * TILES + t
                    if i >= 4:
                        pe.wait_ge(out_done, i - 3)
                    for k in range(DK):
                        mm = nc.tensor.matmul(ps[:, i % 4, 0:chunk], hT[:, k, t * P:(t + 1) * P], w[:, n % 2, k, :],
                                              start=(k == 0), stop=(k == DK - 1))
                    mm.then_inc(mm_done, 1)

        @block.scalar
        def _(act):
            for n in range(n_chunks):
                for t in range(TILES):
                    i = n * TILES + t
                    act.wait_ge(mm_done, i + 1)
                    nc.scalar.activation(out[:, t, n * chunk:(n + 1) * chunk], ps[:, i % 4, 0:chunk],
                                         ACT.Copy).then_inc(out_done, 1)


def output_stage(nc, env, tag, layer, rows, w_dram):
    x, ident = env["x"], env["ident"]
    base = layer * MODW + 2 * D
    with Stage(nc, tag) as s:
        w = s.sb("w", [P, DK, D])
        g = s.sb("gate", [P, 2, D])
        rT = s.sb("rT", [P, 2, DK, P])
        tmp = s.sb("tmp", [P, D])
        pt = s.ps("pt", [P, 2, D])
        po = s.ps("po", [P, 2, D])
        w_in, g_in, tr_done, rT_done = s.sem("w_in"), s.sem("g_in"), s.sem("tr_done"), s.sem("rT_done")
        mm_done, gated, added = s.sem("mm_done"), s.sem("gated"), s.sem("added")
        block = s.stack.enter_context(nc.Block())

        @block.sync
        def _(sp):
            sp.dma_start(w[:], w_dram.rearrange("(k p) n -> p k n", p=P)).then_inc(w_in, 16)
            for c in range(2):
                sp.dma_start(g[:, c, :], broadcast_row(env["mods"][c, base:base + D])).then_inc(g_in, 16)

        @block.tensor
        def _(pe):
            def turn(t):
                if t >= 2:
                    pe.wait_ge(rT_done, t - 1)
                for k in range(DK):
                    mm = nc.tensor.transpose(pt[:, t % 2, k * P:(k + 1) * P], rows[:, t, k * P:(k + 1) * P], ident[:])
                mm.then_inc(tr_done, 1)

            turn(0)
            pe.wait_ge(w_in, 16)
            for t in range(TILES):
                if t + 1 < TILES:
                    turn(t + 1)
                pe.wait_ge(rT_done, t + 1)
                if t >= 2:
                    pe.wait_ge(gated, t - 1)
                for n in range(2):
                    for k in range(DK):
                        mm = nc.tensor.matmul(po[:, t % 2, n * 512:(n + 1) * 512], rT[:, t % 2, k, :],
                                              w[:, k, n * 512:(n + 1) * 512], start=(k == 0), stop=(k == DK - 1))
                mm.then_inc(mm_done, 1)

        @block.scalar
        def _(act):
            for t in range(TILES):
                act.wait_ge(tr_done, t + 1)
                if t >= 2:
                    act.wait_ge(mm_done, t - 1)
                nc.scalar.activation(rT[:, t % 2], pt[:, t % 2, :].rearrange("p (k n) -> p k n", k=DK),
                                     ACT.Copy).then_inc(rT_done, 1)

        @block.vector
        def _(dve):
            dve.wait_ge(g_in, 32)
            for t in range(TILES):
                c = 0 if t < PROMPT_TILES else 1
                dve.wait_ge(mm_done, t + 1)
                if t:
                    dve.wait_ge(added, t)
                nc.vector.tensor_tensor(tmp[:], po[:, t % 2, :], g[:, c, :], ALU.mult).then_inc(gated, 1)
                dve.wait_ge(gated, t + 1)
                nc.vector.tensor_tensor(x[:, t, :], x[:, t, :], tmp[:], ALU.add).then_inc(added, 1)


def decay_stage(nc, a, env, pr, la, st, wsum_key):
    with Stage(nc, "decay") as s:
        wz = s.sb("wz", [2 * LOWRANK + 1, 2 * QK])
        zT = s.sb("zT", [2 * LOWRANK + 1, P])
        sixteenth = s.sb("sixteenth", [P, 1])
        u = s.sb("u", [P, 2 * QK])
        kx = s.sb("kx", [P, 2, QK])
        ku = s.sb("ku", [P, 2, QK])
        eb = s.sb("eb", [P, TILES, 4])
        cs = s.sb("cs", [P, TILES, 4, DV])
        pz, pl, pk, pb, pc = (s.ps(n, [P, 512]) for n in ("pz", "pl", "pk", "pb", "pc"))
        wz_clear, wz_in, st_in, st_out = s.sem("wz_clear"), s.sem("wz_in"), s.sem("st_in"), s.sem("st_out")
        zt_tr, zt_done, z_mm, l_done, la_done = (s.sem(n) for n in ("zt_tr", "zt_done", "z_mm", "l_done", "la_done"))
        k_mm, kx_done, ku_done, b_mm, eb_done, c_mm, c_done = (
            s.sem(n) for n in ("k_mm", "kx_done", "ku_done", "b_mm", "eb_done", "c_mm", "c_done"))
        act_order, dve_order = s.sem("act_order"), s.sem("dve_order")
        block = s.stack.enter_context(nc.Block())

        @block.sync
        def _(sp):
            sp.wait_ge(wz_clear, 3)
            sp.dma_start(wz[0:LOWRANK, 0:QK], a["l0_w_alpha_f"]).then_inc(wz_in, 16)
            sp.dma_start(wz[LOWRANK:2 * LOWRANK, QK:2 * QK], a["l0_w_alpha_b"]).then_inc(wz_in, 16)
            sp.dma_start(wz[2 * LOWRANK:, 0:QK], a["l0_b_alpha_f"].unsqueeze(0)).then_inc(wz_in, 16)
            sp.dma_start(wz[2 * LOWRANK:, QK:2 * QK], a["l0_b_alpha_b"].unsqueeze(0)).then_inc(wz_in, 16)
            sp.dma_start(wsum_key[:], a["k_key_sums"]).then_inc(wz_in, 16)
            for d, first in ((0, 0), (1, LATENT_TILES - 1)):
                sp.dma_start(st[:, d, first], a["state_l0_gla"][0, d].rearrange("(hh hp) k v -> (hp k) hh v", hp=2)
                             ).then_inc(st_in, 16)
            sp.wait_ge(c_done, 1)
            for d in range(2):
                sp.dma_start(a["out_state"][0, d].rearrange("(hh hp) k v -> (hp k) hh v", hp=2),
                             cs[:, 0, 2 * d:2 * d + 2, :]).then_inc(st_out, 16)
            sp.wait_ge(st_out, 32)

        @block.tensor
        def _(pe):
            pe.wait_ge(wz_in, 80)
            for t in range(TILES):
                if t:
                    pe.wait_ge(zt_done, t)
                nc.tensor.transpose(pz[0:2 * LOWRANK, 0:P], pr[:, t, Z0:Z0 + 2 * LOWRANK], env["ident"][:]).then_inc(zt_tr, 1)
                pe.wait_ge(zt_done, t + 1)
                if t:
                    pe.wait_ge(la_done, t)
                nc.tensor.matmul(pl[:], zT[:], wz[:], start=True, stop=True).then_inc(z_mm, 1)
                pe.wait_ge(la_done, t + 1)
                if t:
                    pe.wait_ge(kx_done, t)
                    pe.wait_ge(eb_done, t)
                for d in range(2):
                    mm = nc.tensor.matmul(pk[:, d * QK:(d + 1) * QK], wsum_key[:, d, :], la[:, t, d * QK:(d + 1) * QK],
                                          start=True, stop=True)
                mm.then_inc(k_mm, 1)
                for j in range(4):
                    mm = nc.tensor.matmul(pb[:, j:j + 1], la[:, t, j * P:(j + 1) * P], sixteenth[:], start=True, stop=True)
                mm.then_inc(b_mm, 1)
                pe.wait_ge(ku_done, t + 1)
                if t:
                    pe.wait_ge(c_done, t)
                for d in range(2):
                    for head in range(HEADS0):
                        lo = 64 * (head % 2)
                        j = 2 * d + head // 2
                        mm = nc.tensor.matmul(pc[lo:lo + 64, j * DV:(j + 1) * DV], ku[:, d, head * DKH:(head + 1) * DKH],
                                              pr[:, t, V0 + head * DV:V0 + (head + 1) * DV], start=True, stop=True)
                mm.then_inc(c_mm, 1)

        @block.scalar
        def _(act):
            order = Order(act, act_order)
            act.wait_ge(wz_clear, 3)
            for t in range(TILES):
                act.wait_ge(zt_tr, t + 1)
                if t:
                    act.wait_ge(z_mm, t)
                nc.scalar.activation(zT[0:2 * LOWRANK, :], pz[0:2 * LOWRANK, 0:P], ACT.Copy).then_inc(zt_done, 1)
                act.wait_ge(z_mm, t + 1)
                if t:
                    act.wait_ge(la_done, t)
                order(nc.scalar.activation(u[:], pl[:], ACT.Abs))
                order(nc.scalar.activation(u[:], u[:], ACT.Exp, scale=-1.0))
                nc.scalar.activation(u[:], u[:], ACT.Ln, bias=1.0).then_inc(l_done, 1)
                act.wait_ge(k_mm, t + 1)
                if t:
                    act.wait_ge(ku_done, t)
                nc.scalar.activation(kx[:].rearrange("p d n -> p (d n)"), pk[:], ACT.Exp).then_inc(kx_done, 1)
                act.wait_ge(b_mm, t + 1)
                nc.scalar.activation(eb[:, t, :], pb[:, 0:4], ACT.Exp).then_inc(eb_done, 1)

        @block.vector
        def _(dve):
            order = Order(dve, dve_order)
            nc.vector.memset(wz[:], 0.0).then_inc(wz_clear, 1)
            nc.vector.memset(zT[2 * LOWRANK:, :], 1.0).then_inc(wz_clear, 1)
            nc.vector.memset(sixteenth[:], 1.0 / 16).then_inc(wz_clear, 1)
            for t in range(TILES):
                dve.wait_ge(l_done, t + 1)
                nc.vector.scalar_tensor_tensor(la[:, t, :], pl[:], 0.0, u[:], ALU.min, ALU.subtract).then_inc(la_done, 1)
                dve.wait_ge(kx_done, t + 1)
                if t:
                    dve.wait_ge(c_mm, t)
                k_rows = pr[:, t, K0:K0 + QK].unsqueeze(1).to_broadcast([P, 2, QK])
                nc.vector.tensor_tensor(ku[:], kx[:], k_rows, ALU.mult).then_inc(ku_done, 1)
                dve.wait_ge(c_mm, t + 1)
                nc.vector.tensor_copy(cs[:, t].rearrange("p j v -> p (j v)"), pc[:]).then_inc(c_done, 1)
            dve.wait_ge(st_in, 32)
            dve.wait_ge(eb_done, TILES)
            dve.wait_ge(c_done, TILES)
            for i in range(LATENT_TILES - 1):
                for d, (src, dst) in enumerate(((i, i + 1), (LATENT_TILES - 1 - i, LATENT_TILES - 2 - i))):
                    for hh in range(2):
                        j = 2 * d + hh
                        order(nc.vector.scalar_tensor_tensor(st[:, d, dst, hh, :], st[:, d, src, hh, :],
                                                             eb[:, PROMPT_TILES + src, j:j + 1],
                                                             cs[:, PROMPT_TILES + src, j, :], ALU.mult, ALU.add))


def gla_stage(nc, a, env, pr, la, st, mix):
    HALVES = 2
    UN = TILES * HALVES
    SL = LEVELS + 1
    BATCH = 4
    BATCHES = -(-(1 + 2 * LEVELS) // BATCH)
    SC = 1 + 2 * LEVELS
    with Stage(nc, "gla") as s:
        wsum = s.sb("wsum", [P, 2, SL, P])
        mask = s.sb("mask", [P, 2, LEVELS, P], I32)
        gn = s.sb("gn", [P, DV])
        qkT = s.sb("qkT", [P, 4, P])
        e = s.sb("e", [P, 2, SL, P])
        qe = s.sb("qe", [P, 2, SL, P])
        ke = s.sb("ke", [P, 2, SL, P])
        sc = s.sb("sc", [P, 2, P])
        sq = s.sb("sq", [P, VW])
        ss = s.sb("ss", [P, HEADS0])
        sg = s.sb("sg", [P, VW])
        pd = s.ps("pd", [P, SL * P])
        pt = pd[:, 0:4 * P].rearrange("p (j n) -> p j n", j=4)
        pscore = s.ps("pscore", [P, 2, 2, BATCH, P])
        po = s.ps("po", [P, 2, 512])
        po_heads = po[:].rearrange("p b (hf v) -> p hf b v", v=DV)[:, 0:2]
        const_in, tr_done, qkT_done, d_mm, e_done, qe_done, ke_done = (
            s.sem(n) for n in ("const_in", "tr_done", "qkT_done", "d_mm", "e_done", "qe_done", "ke_done"))
        score_mm, score_used, o_mm, sq_done, mean_done, sqrt_done, r_exp, mix_done = (
            s.sem(n) for n in ("score_mm", "score_used", "o_mm", "sq_done", "mean_done", "sqrt_done", "r_exp", "mix_done"))
        dve_order = s.sem("dve_order")
        block = s.stack.enter_context(nc.Block())

        @block.sync
        def _(sp):
            sp.dma_start(wsum[:], a["k_level_sums"]).then_inc(const_in, 16)
            sp.dma_start(mask[:], a["k_level_masks"]).then_inc(const_in, 16)
            sp.dma_start(gn[:], broadcast_row(a["l0_gla_norm"])).then_inc(const_in, 16)

        @block.tensor
        def _(pe):
            pe.wait_ge(const_in, 48)
            for n in range(UN):
                t, half = divmod(n, HALVES)
                if n:
                    pe.wait_ge(e_done, 2 * n)
                if half == 0:
                    for j in range(4):
                        mm = nc.tensor.transpose(pt[:, j, :], pr[:, t, j * P:(j + 1) * P], env["ident"][:])
                    mm.then_inc(tr_done, 1)
                    pe.wait_ge(qkT_done, t + 1)
                for d in range(2):
                    if d:
                        pe.wait_ge(e_done, 2 * n + 1)
                    for c in range(2):
                        mm = nc.tensor.matmul(pd[:, c * 512:(c + 1) * 512], la[:, t, d * QK + half * P:d * QK + (half + 1) * P],
                                              wsum[:, d].rearrange("p l n -> p (l n)")[:, c * 512:(c + 1) * 512],
                                              start=True, stop=True)
                    mm.then_inc(d_mm, 1)
                for jb in range(BATCHES):
                    batch = n * BATCHES + jb
                    if jb == 0:
                        pe.wait_ge(qe_done, n + 1)
                        pe.wait_ge(ke_done, n + 1)
                    if batch >= 2:
                        pe.wait_ge(score_used, batch - 1)
                    for j in range(jb * BATCH, min(SC, (jb + 1) * BATCH)):
                        for hh in range(2):
                            lo = 64 * hh
                            if j == 0:
                                keys, queries = qkT[lo:lo + 64, 2 + half, :], qkT[lo:lo + 64, half, :]
                            else:
                                d, lv = divmod(j - 1, LEVELS)
                                keys, queries = ke[lo:lo + 64, d, lv, :], qe[lo:lo + 64, d, lv, :]
                            mm = nc.tensor.matmul(pscore[:, batch % 2, hh, j % BATCH, :], keys, queries, start=True, stop=True)
                    mm.then_inc(score_mm, 1)
                pe.wait_ge(score_used, (n + 1) * BATCHES)
                if half == 0 and t:
                    pe.wait_ge(mix_done, t)
                for hh in range(2):
                    head, lo = 2 * half + hh, 64 * hh
                    latent = t >= PROMPT_TILES
                    mm = nc.tensor.matmul(po[:, hh, half * DV:(half + 1) * DV], sc[:, hh, :], pr[:, t, V0 + head * DV:V0 + (head + 1) * DV],
                                          start=True, stop=not latent)
                    if latent:
                        for d in range(2):
                            mm = nc.tensor.matmul(po[:, hh, half * DV:(half + 1) * DV], qe[lo:lo + 64, d, LEVELS, :],
                                                  st[lo:lo + 64, d, t - PROMPT_TILES, half, :], start=False, stop=(d == 1))
                mm.then_inc(o_mm, 1)

        @block.scalar
        def _(act):
            for n in range(UN):
                t, half = divmod(n, HALVES)
                if half == 0:
                    act.wait_ge(tr_done, t + 1)
                    if t:
                        act.wait_ge(ke_done, n)
                        act.wait_ge(qe_done, n)
                        act.wait_ge(o_mm, n)
                    nc.scalar.activation(qkT[:, 0:2, :], pt[:, 0:2, :], ACT.Copy, scale=DKH ** -0.5)
                    nc.scalar.activation(qkT[:, 2:4, :], pt[:, 2:4, :], ACT.Copy).then_inc(qkT_done, 1)
                if n:
                    act.wait_ge(qe_done, n)
                    act.wait_ge(ke_done, n)
                for d in range(2):
                    act.wait_ge(d_mm, 2 * n + d + 1)
                    nc.scalar.activation(e[:, d].rearrange("p l n -> p (l n)"), pd[:], ACT.Exp).then_inc(e_done, 1)
                if half == 1:
                    act.wait_ge(o_mm, n + 1)
                    if t:
                        act.wait_ge(mix_done, t)
                    nc.scalar.activation(sq[:].rearrange("p (hf b v) -> p hf b v", hf=2, b=2), po_heads, ACT.Square).then_inc(sq_done, 1)
                    nc.scalar.activation(sg[:], pr[:, t, R0:R0 + VW], ACT.Exp, scale=-1.0).then_inc(r_exp, 1)
                    act.wait_ge(mean_done, t + 1)
                    nc.scalar.activation(ss[:], ss[:], ACT.Sqrt).then_inc(sqrt_done, 1)

        @block.gpsimd
        def _(pool):
            for n in range(UN):
                t, half = divmod(n, HALVES)
                pool.wait_ge(e_done, 2 * n + 2)
                pool.wait_ge(qkT_done, t + 1)
                if n:
                    pool.wait_ge(o_mm, n)
                kk = qkT[:, 2 + half, :].unsqueeze(1).to_broadcast([P, 2 * SL, P])
                nc.gpsimd.tensor_tensor(ke[:].rearrange("p d l n -> p (d l) n"), e[:].rearrange("p d l n -> p (d l) n"), kk,
                                        ALU.mult).then_inc(ke_done, 1)

        @block.vector
        def _(dve):
            order = Order(dve, dve_order)
            dve.wait_ge(const_in, 48)
            for n in range(UN):
                t, half = divmod(n, HALVES)
                dve.wait_ge(e_done, 2 * n + 2)
                dve.wait_ge(qkT_done, t + 1)
                if n:
                    dve.wait_ge(o_mm, n)
                qq = qkT[:, half, :].unsqueeze(1).to_broadcast([P, 2 * SL, P])
                nc.vector.tensor_tensor(qe[:].rearrange("p d l n -> p (d l) n"), e[:].rearrange("p d l n -> p (d l) n"), qq,
                                        ALU.mult).then_inc(qe_done, 1)
                for j in range(SC):
                    batch = n * BATCHES + j // BATCH
                    if j % BATCH == 0:
                        dve.wait_ge(score_mm, batch + 1)
                    src = pscore[:, batch % 2, :, j % BATCH, :]
                    if j == 0:
                        x = nc.vector.tensor_scalar(sc[:], src, 2.0, None, ALU.mult)
                    else:
                        d, lv = divmod(j - 1, LEVELS)
                        x = nc.vector.copy_predicated(sc[:], mask[:, d, lv, :].unsqueeze(1).to_broadcast([P, 2, P]), src)
                    if j % BATCH == BATCH - 1 or j == SC - 1:
                        x.then_inc(score_used, 1)
                        dve.wait_ge(score_used, batch + 1)
                    else:
                        order(x)
                if half == 1:
                    dve.wait_ge(sq_done, t + 1)
                    order(nc.vector.tensor_reduce(ss[:], sq[:].rearrange("p (h v) -> p h v", h=HEADS0), AX.X, ALU.add))
                    nc.vector.tensor_scalar(ss[:], ss[:], 1.0 / DV, EPS, ALU.mult, ALU.add).then_inc(mean_done, 1)
                    dve.wait_ge(r_exp, t + 1)
                    order(nc.vector.tensor_scalar_add(sg[:], sg[:], 1.0))
                    order(nc.vector.reciprocal(sg[:], sg[:]))
                    order(nc.vector.tensor_tensor(sg[:], sg[:], pr[:, t, R0:R0 + VW], ALU.mult))
                    sg3 = sg[:].rearrange("p (h v) -> p h v", h=HEADS0)
                    order(nc.vector.tensor_tensor(sg3, sg3, gn[:].unsqueeze(1).to_broadcast([P, HEADS0, DV]), ALU.mult))
                    dve.wait_ge(sqrt_done, t + 1)
                    order(nc.vector.reciprocal(ss[:], ss[:]))
                    rstd = ss[:].rearrange("p (hf b) -> p hf b", hf=2).unsqueeze(3).to_broadcast([P, 2, 2, DV])
                    order(nc.vector.tensor_tensor(sq[:].rearrange("p (hf b v) -> p hf b v", hf=2, b=2), po_heads, rstd, ALU.mult))
                    nc.vector.tensor_tensor(mix[:, t, 0:VW], sq[:], sg[:], ALU.mult).then_inc(mix_done, 1)


def pool_stage(nc, a, pr, mix):
    G = len(POOL_WINDOWS)
    with Stage(nc, "pool") as s:
        band = s.sb("band", [P, 6, G, P])
        pw = s.sb("pw", [P, G, P])
        psc = s.sb("psc", [P, VW])
        dT = s.sb("dT", [P, 2, G, P])
        pd = s.ps("pd", [P, 2, G, P])
        py = s.ps("py", [P, 2, VW])
        const_in, d_mm, d_done, y_mm, y_done = (s.sem(n) for n in ("const_in", "d_mm", "d_done", "y_mm", "y_done"))
        block = s.stack.enter_context(nc.Block())

        @block.sync
        def _(sp):
            sp.dma_start(band[:], a["k_pool"]).then_inc(const_in, 16)
            sp.dma_start(pw[:], a["l0_pool_w"].rearrange("g i o -> i g o")).then_inc(const_in, 16)
            sp.dma_start(psc[:], broadcast_row(a["l0_pool_scale"])).then_inc(const_in, 16)

        @block.tensor
        def _(pe):
            pe.wait_ge(const_in, 48)
            for t in range(TILES):
                if t == 0:
                    parts = [(0, 0)]
                else:
                    own = 1 if t == PROMPT_TILES else (3 if t == TILES - 1 else 2)
                    parts = [(t, own)]
                    if t > PROMPT_TILES:
                        parts.append((t - 1, 4))
                    if t < TILES - 1:
                        parts.append((t + 1, 5))
                if t >= 2:
                    pe.wait_ge(d_done, t - 1)
                for g in range(G):
                    for i, (src, v) in enumerate(parts):
                        mm = nc.tensor.matmul(pd[:, t % 2, g, :], pr[:, src, PIN0 + g * P:PIN0 + (g + 1) * P], band[:, v, g, :],
                                              start=(i == 0), stop=(i == len(parts) - 1))
                mm.then_inc(d_mm, 1)
                pe.wait_ge(d_done, t + 1)
                if t >= 2:
                    pe.wait_ge(y_done, t - 1)
                for g in range(G):
                    mm = nc.tensor.matmul(py[:, t % 2, g * P:(g + 1) * P], dT[:, t % 2, g, :], pw[:, g, :], start=True, stop=True)
                mm.then_inc(y_mm, 1)

        @block.scalar
        def _(act):
            for t in range(TILES):
                act.wait_ge(d_mm, t + 1)
                if t >= 2:
                    act.wait_ge(y_mm, t - 1)
                nc.scalar.activation(dT[:, t % 2], pd[:, t % 2], ACT.Copy).then_inc(d_done, 1)

        @block.vector
        def _(dve):
            dve.wait_ge(const_in, 48)
            for t in range(TILES):
                dve.wait_ge(y_mm, t + 1)
                nc.vector.tensor_tensor(mix[:, t, VW:], py[:, t % 2, :], psc[:], ALU.mult).then_inc(y_done, 1)


def qk_stage(nc, a, env, pr, qT, kT, vc):
    QKH = QH + KVH
    W = QKH * HD
    with Stage(nc, "qk") as s:
        gain = s.sb("gain", [P, 2, HD])
        rope = s.sb("rope", [P, 2, LATENT_TILES, HD])
        kc = s.sb("kc", [P, KVH, HD])
        sq = s.sb("sq", [P, W])
        t2 = s.sb("t2", [P, W])
        ss = s.sb("ss", [P, QKH])
        kd = s.sb("kd", [P, KVH, 2, HD])
        pq = s.ps("pq", [P, 8, P])
        pk = s.ps("pk", [P, KVH, P])
        const_in, stored, sq_done, mean_done, sqrt_done = (s.sem(n) for n in ("const_in", "stored", "sq_done", "mean_done", "sqrt_done"))
        normed, kd_done, q_tr, k_tr, q_done, k_done, dve_order = (
            s.sem(n) for n in ("normed", "kd_done", "q_tr", "k_tr", "q_done", "k_done", "dve_order"))
        block = s.stack.enter_context(nc.Block())

        @block.sync
        def _(sp):
            sp.dma_start(gain[:, 0, :], broadcast_row(a["l1_q_norm"])).then_inc(const_in, 16)
            sp.dma_start(gain[:, 1, :], broadcast_row(a["l1_k_norm"])).then_inc(const_in, 16)
            sp.dma_start(rope[:], a["k_rope"]).then_inc(const_in, 16)
            sp.dma_start(kc[:], a["cache_l1_k"][0]).then_inc(const_in, 16)
            sp.dma_start(vc[:], a["cache_l1_v"][0].rearrange("t k d -> t (k d)")).then_inc(const_in, 16)
            sp.dma_start(a["out_v"][0].rearrange("t k d -> t (k d)"), pr[:, 0, W:]).then_inc(stored, 16)
            sp.wait_ge(normed, 1)
            sp.dma_start(a["out_k"][0].rearrange("t k d -> t (k d)"), pr[:, 0, QH * HD:W]).then_inc(stored, 16)
            sp.wait_ge(stored, 32)
            sp.wait_ge(const_in, 80)

        @block.scalar
        def _(act):
            for t in range(TILES):
                if t:
                    act.wait_ge(normed, t)
                nc.scalar.activation(sq[:], pr[:, t, 0:W], ACT.Square).then_inc(sq_done, 1)
                act.wait_ge(mean_done, t + 1)
                nc.scalar.activation(ss[:], ss[:], ACT.Sqrt).then_inc(sqrt_done, 1)
                act.wait_ge(q_tr, t + 1)
                nc.scalar.activation(qT[:, t], pq[:], ACT.Copy, scale=HD ** -0.5).then_inc(q_done, 1)
                act.wait_ge(k_tr, t + 1)
                nc.scalar.activation(kT[:, :, t, :], pk[:], ACT.Copy).then_inc(k_done, 1)
            act.wait_ge(k_tr, TILES + 1)
            nc.scalar.activation(kT[:, :, TILES, :], pk[:], ACT.Copy).then_inc(k_done, 1)

        @block.vector
        def _(dve):
            order = Order(dve, dve_order)
            dve.wait_ge(const_in, 80)
            for t in range(TILES):
                qk = pr[:, t, 0:W].rearrange("p (h d) -> p h d", d=HD)
                sq3 = sq[:].rearrange("p (h d) -> p h d", d=HD)
                t23 = t2[:].rearrange("p (h d) -> p h d", d=HD)
                dve.wait_ge(sq_done, t + 1)
                order(nc.vector.tensor_reduce(ss[:], sq3, AX.X, ALU.add))
                nc.vector.tensor_scalar(ss[:], ss[:], 1.0 / HD, EPS, ALU.mult, ALU.add).then_inc(mean_done, 1)
                dve.wait_ge(sqrt_done, t + 1)
                order(nc.vector.reciprocal(ss[:], ss[:]))
                order(nc.vector.tensor_tensor(qk, qk, ss[:].unsqueeze(2).to_broadcast([P, QKH, HD]), ALU.mult))
                order(nc.vector.tensor_tensor(qk[:, 0:QH], qk[:, 0:QH], gain[:, 0:1, :].to_broadcast([P, QH, HD]), ALU.mult))
                order(nc.vector.tensor_tensor(qk[:, QH:], qk[:, QH:], gain[:, 1:2, :].to_broadcast([P, KVH, HD]), ALU.mult))
                if t >= PROMPT_TILES:
                    lt = t - PROMPT_TILES
                    for x2 in range(2):
                        def part(v, j):
                            return v.rearrange("p h (g j e) -> p h g j e", g=2, j=2)[:, :, :, j, :]
                        sin = rope[:, 1, lt:lt + 1, :].rearrange("p o (g j e) -> p o g j e", g=2, j=2)[:, :, :, x2, :]
                        order(nc.vector.tensor_tensor(part(t23, x2), part(qk, 1 - x2),
                                                      sin.to_broadcast([P, QKH, 2, HD // 4]), ALU.mult))
                    order(nc.vector.tensor_tensor(qk, qk, rope[:, 0, lt:lt + 1, :].to_broadcast([P, QKH, HD]), ALU.mult))
                    order(nc.vector.tensor_tensor(qk, qk, t23, ALU.add))
                if t:
                    dve.wait_ge(k_tr, t)
                for dup in range(2):
                    i = nc.vector.tensor_copy(kd[:, :, dup, :], qk[:, QH:])
                i.then_inc(normed, 1)
            dve.wait_ge(k_tr, TILES)
            for dup in range(2):
                i = nc.vector.tensor_copy(kd[:, :, dup, :], kc[:])
            i.then_inc(normed, 1)

        @block.tensor
        def _(pe):
            for t in range(TILES + 1):
                pe.wait_ge(normed, t + 1)
                if t < TILES:
                    if t:
                        pe.wait_ge(q_done, t)
                    for j in range(8):
                        mm = nc.tensor.transpose(pq[:, j, :], pr[:, t, j * P:(j + 1) * P], env["ident"][:])
                    mm.then_inc(q_tr, 1)
                if t:
                    pe.wait_ge(k_done, t)
                for j in range(KVH):
                    mm = nc.tensor.transpose(pk[:, j, :], kd[:, j].rearrange("p u d -> p (u d)"), env["ident"][:])
                mm.then_inc(k_tr, 1)


def attention_stage(nc, a, env, pr, qT, kT, vc, rows):
    V1 = (QH + KVH) * HD
    UN = TILES * QH
    CTX = TILES

    def keys_of(t):
        if t < PROMPT_TILES:
            return [0], 1
        if t == PROMPT_TILES:
            return [t, t + 1, CTX], 1
        if t == TILES - 1:
            return [t - 1, t, CTX], 4
        return [t - 1, t, t + 1, CTX], 0

    with Stage(nc, "att") as s:
        win = s.sb("win", [P, 7, P])
        sink = s.sb("sink", [P, QH])
        sc = s.sb("sc", [P, 2, 4 * P])
        pT = s.sb("pT", [P, 2, 4, P])
        mx = s.sb("mx", [P, 2])
        den = s.sb("den", [P, 2, QH])
        es = s.sb("es", [P, 2, QH])
        pscore = s.ps("pscore", [P, 2, 4 * P])
        ptr = s.ps("ptr", [P, 2, 4, P])
        po = s.ps("po", [P, 2, QH, HD])
        const_in, s_mm, max_done, neg_done, exp_done, tr_done, pT_done, o_mm, es_done, row_done, dve_order = (
            s.sem(n) for n in ("const_in", "s_mm", "max_done", "neg_done", "exp_done", "tr_done", "pT_done", "o_mm",
                               "es_done", "row_done", "dve_order"))
        block = s.stack.enter_context(nc.Block())

        @block.sync
        def _(sp):
            sp.dma_start(win[:], a["k_window"]).then_inc(const_in, 16)
            sp.dma_start(sink[:], broadcast_row(a["l1_sink"])).then_inc(const_in, 16)
            sp.wait_ge(const_in, 32)

        @block.tensor
        def _(pe):
            def scores(n):
                t, head = divmod(n, QH)
                lo, g = 64 * (head % 2), head // (QH // KVH)
                keys, _ = keys_of(t)
                if n >= 2:
                    pe.wait_ge(max_done, n - 1)
                q = qT[lo:lo + 64, t, head // 2, :]
                local = [k for k in keys if k != CTX]
                mm = nc.tensor.matmul(pscore[:, n % 2, 0:len(local) * P], q,
                                      kT[lo:lo + 64, g, local[0]:local[-1] + 1, :].rearrange("p t n -> p (t n)"),
                                      start=True, stop=True)
                if CTX in keys:
                    mm = nc.tensor.matmul(pscore[:, n % 2, len(local) * P:len(keys) * P], q, kT[lo:lo + 64, g, CTX, :],
                                          start=True, stop=True)
                mm.then_inc(s_mm, 1)

            def turn(n):
                keys, _ = keys_of(n // QH)
                pe.wait_ge(exp_done, n + 1)
                if n >= 2:
                    pe.wait_ge(pT_done, n - 1)
                for j in range(len(keys)):
                    mm = nc.tensor.transpose(ptr[:, n % 2, j, :], sc[:, n % 2, j * P:(j + 1) * P], env["ident"][:])
                mm.then_inc(tr_done, 1)

            def values(n):
                t, head = divmod(n, QH)
                g = head // (QH // KVH)
                keys, _ = keys_of(t)
                pe.wait_ge(pT_done, n + 1)
                if head == 0 and t >= 2:
                    pe.wait_ge(row_done, t - 1)
                for j, k in enumerate(keys):
                    v = vc[:, g * HD:(g + 1) * HD] if k == CTX else pr[:, k, V1 + g * HD:V1 + (g + 1) * HD]
                    mm = nc.tensor.matmul(po[:, t % 2, head, :], pT[:, n % 2, j, :], v, start=(j == 0), stop=(j == len(keys) - 1))
                mm.then_inc(o_mm, 1)

            for i in range(UN + 2):
                if i < UN:
                    scores(i)
                if 1 <= i <= UN:
                    turn(i - 1)
                if i >= 2:
                    values(i - 2)

        @block.scalar
        def _(act):
            for n in range(UN):
                t, head = divmod(n, QH)
                w = len(keys_of(t)[0]) * P
                act.wait_ge(neg_done, n + 1)
                if head == 0 and t >= 2:
                    act.wait_ge(row_done, t - 1)
                nc.scalar.activation(sc[:, n % 2, 0:w], sc[:, n % 2, 0:w], ACT.Exp, bias=mx[:, n % 2:n % 2 + 1],
                                     accum_out=den[:, t % 2, head:head + 1]).then_inc(exp_done, 1)
                nc.scalar.activation(es[:, t % 2, head:head + 1], sink[:, head:head + 1], ACT.Exp,
                                     bias=mx[:, n % 2:n % 2 + 1]).then_inc(es_done, 1)

        @block.vector
        def _(dve):
            order = Order(dve, dve_order)
            dve.wait_ge(const_in, 32)
            for n in range(UN + 2):
                if n < UN:
                    t, head = divmod(n, QH)
                    keys, m0 = keys_of(t)
                    w = len(keys) * P
                    dve.wait_ge(s_mm, n + 1)
                    if n >= 2:
                        dve.wait_ge(tr_done, n - 1)
                        dve.wait_ge(es_done, n - 1)
                    nc.vector.tensor_tensor_reduce(sc[:, n % 2, 0:w], pscore[:, n % 2, 0:w],
                                                   win[:, m0:m0 + len(keys), :].rearrange("p t n -> p (t n)"), 1.0,
                                                   sink[:, head:head + 1], ALU.add, ALU.max,
                                                   mx[:, n % 2:n % 2 + 1]).then_inc(max_done, 1)
                    dve.wait_ge(max_done, n + 1)
                    nc.vector.tensor_scalar(mx[:, n % 2:n % 2 + 1], mx[:, n % 2:n % 2 + 1], -1.0, None,
                                            ALU.mult).then_inc(neg_done, 1)
                if n >= 1 and n <= UN:
                    u = n - 1
                    keys, _ = keys_of(u // QH)
                    dve.wait_ge(tr_done, u + 1)
                    if u >= 2:
                        dve.wait_ge(o_mm, u - 1)
                    nc.vector.tensor_copy(pT[:, u % 2, 0:len(keys), :], ptr[:, u % 2, 0:len(keys), :]).then_inc(pT_done, 1)
                if n >= 2 and (n - 2) % QH == QH - 1:
                    t = (n - 2) // QH
                    dve.wait_ge(o_mm, (t + 1) * QH)
                    dve.wait_ge(es_done, (t + 1) * QH)
                    order(nc.vector.tensor_tensor(den[:, t % 2], den[:, t % 2], es[:, t % 2], ALU.add))
                    order(nc.vector.reciprocal(den[:, t % 2], den[:, t % 2]))
                    nc.vector.tensor_tensor(rows[:, t, :].rearrange("p (h d) -> p h d", d=HD), po[:, t % 2],
                                            den[:, t % 2].unsqueeze(2).to_broadcast([P, QH, HD]), ALU.mult).then_inc(row_done, 1)


def select_stage(nc, a, env, tag, layer, hT, experts, gates):
    HC = 2 * PH
    SLOT = 4
    LOW = -3.0e38
    with Stage(nc, tag) as s:
        w = s.sb("w", [P, SLOT, DK, P])
        keys = s.sb("keys", [P, HC, NKEYS])
        qT = s.sb("qT", [P, 2, TOK])
        rest = s.sb("rest", [P, TILES, NKEYS])
        v1 = s.sb("v1", [P, TILES, TOPK])
        i1 = s.sb("i1", [P, TILES, TOPK], U32)
        vals = s.sb("vals", [P, TILES, HC, TOPK])
        idxf = s.sb("idxf", [P, TILES, HC, TOPK])
        iota = s.sb("iota", [P, TOPK])
        cand = s.sb("cand", [P, PH, TOPK * TOPK])
        cand2 = s.sb("cand2", [P, PH, TOPK * TOPK])
        ts = s.sb("ts", [P, PH, TOPK])
        tp = s.sb("tp", [P, PH, TOPK], U32)
        tu = s.sb("tu", [P, PH, TOPK], U32)
        pa = s.sb("pa", [P, 2, PH, TOPK])
        ef = s.sb("ef", [P, 2, PH, TOPK])
        gs = s.sb("gs", [P, PH])
        pq = s.ps("pq", [P, 2, 1024])
        pscore = s.ps("pscore", [P, 2, 1024])
        keys_in = s.sem("keys_in")
        w_in = [s.sem(f"w_in{i}") for i in range(SLOT)]
        w_free, q_mm, qT_done, s_mm, used = (s.sem(n) for n in ("w_free", "q_mm", "qT_done", "s_mm", "used"))
        dve_order, waited, shifted, exp_done = (s.sem(n) for n in ("dve_order", "waited", "shifted", "exp_done"))
        block = s.stack.enter_context(nc.Block())
        STEPS = 5

        @block.sync
        def _(sp):
            sp.dma_start(keys[:], a[f"l{layer}_peer_keys"]).then_inc(keys_in, 16)
            sp.dma_start(iota[:], a["k_iota"]).then_inc(keys_in, 16)
            wv = a[f"l{layer}_peer_wq"].rearrange("(k p) n -> p k n", p=P)
            with sp.Fori(0, HC // SLOT) as i:
                for slot in range(SLOT):
                    sp.wait_ge(w_free, i * SLOT + slot + 1)
                    sp.dma_start(w[:, slot], wv[:, :, bass.ds((i * SLOT + slot) * P, P)]).then_inc(w_in[slot], 16)

        @block.tensor
        def _(pe):
            pe.sem_inc(w_free, SLOT)
            pe.sem_inc(q_mm, 1)
            pe.wait_ge(keys_in, 32)
            with pe.Fori(0, HC // SLOT) as i:
                for slot in range(SLOT):
                    n = i * SLOT + slot
                    b = slot % 2
                    pe.wait_ge(w_in[slot], i * 16 + 16)
                    pe.wait_ge(qT_done, n + 1)
                    for k in range(DK):
                        for lo, hi in ((0, 512), (512, TOK)):
                            mm = nc.tensor.matmul(pq[:, b, lo:hi], w[:, slot, k, :], hT[:, k, lo:hi],
                                                  start=(k == 0), stop=(k == DK - 1))
                    mm.then_inc(q_mm, 1)
                    pe.wait_ge(q_mm, n + 2)
                    pe.sem_inc(w_free, 1)
                    pe.wait_ge(qT_done, n + 3)
                    pe.wait_ge(used, n + 1)
                    for t in range(TILES):
                        mm = nc.tensor.matmul(pscore[:, b, t * P:(t + 1) * P], qT[:, b, t * P:(t + 1) * P],
                                              keys[:, bass.ds(n, 1), :].rearrange("p o n -> p (o n)"), start=True, stop=True)
                    mm.then_inc(s_mm, 1)

        @block.scalar
        def _(act):
            act.sem_inc(qT_done, 2)
            act.sem_inc(s_mm, 2)
            with act.Fori(0, HC // SLOT) as i:
                for slot in range(SLOT):
                    n = i * SLOT + slot
                    act.wait_ge(q_mm, n + 2)
                    act.wait_ge(s_mm, n + 1)
                    nc.scalar.activation(qT[:, slot % 2, :], pq[:, slot % 2, 0:TOK], ACT.Copy).then_inc(qT_done, 1)
            with act.Fori(0, TILES) as t:
                act.wait_ge(shifted, t + 1)
                nc.scalar.activation(ts[:], ts[:], ACT.Exp).then_inc(exp_done, 1)

        @block.vector
        def _(dve):
            dve.sem_inc(used, 2)
            with dve.Fori(0, HC // 2) as i:
                for b in range(2):
                    n = 2 * i + b
                    dve.wait_ge(s_mm, n + 3)
                    dve.sem_inc(waited, 1)
                    base = n * STEPS
                    for step in range(STEPS):
                        for t in range(TILES):
                            sc = pscore[:, b, t * P:(t + 1) * P]
                            va, vb = v1[:, t, 0:8], v1[:, t, 8:16]
                            if step == 0:
                                x = nc.vector.max(va, sc)
                            elif step == 1:
                                x = nc.vector.max_index(i1[:, t, 0:8], va, sc)
                            elif step == 2:
                                x = nc.vector.match_replace(rest[:, t, :], va, sc, LOW)
                            elif step == 3:
                                x = nc.vector.max(vb, rest[:, t, :])
                            else:
                                x = nc.vector.max_index(i1[:, t, 8:16], vb, rest[:, t, :])
                        x.then_inc(dve_order, 1)
                        dve.wait_ge(dve_order, base + step + 1)
                        dve.sem_inc(waited, 1)
                    nc.vector.tensor_copy(vals[:, :, bass.ds(n, 1), :].rearrange("p t o k -> p t (o k)"), v1[:])
                    nc.vector.tensor_copy(idxf[:, :, bass.ds(n, 1), :].rearrange("p t o k -> p t (o k)"), i1[:]).then_inc(used, 1)
                    dve.wait_ge(used, n + 3)
            base = HC * STEPS
            CSTEPS = 18
            dve.wait_ge(keys_in, 32)
            with dve.Fori(0, TILES) as t:
                n = [0]

                def order(x):
                    x.then_inc(dve_order, 1)
                    n[0] += 1
                    dve.wait_ge(dve_order, base + t * CSTEPS + n[0])
                    dve.sem_inc(waited, 1)

                def tile(v):
                    return v[:, bass.ds(t, 1)].rearrange("p o c k -> p (o c) k").rearrange("p (h c) k -> p h c k", c=2)
                va, ia = tile(vals), tile(idxf)
                cand4 = cand[:].rearrange("p h (x y) -> p h x y", x=TOPK)
                cand24 = cand2[:].rearrange("p h (x y) -> p h x y", x=TOPK)
                shape = [P, PH, TOPK, TOPK]
                order(nc.vector.tensor_tensor(cand4, va[:, :, 0, :].unsqueeze(3).to_broadcast(shape),
                                              va[:, :, 1, :].unsqueeze(2).to_broadcast(shape), ALU.add))
                for step in range(5):
                    for h in range(PH):
                        if step == 0:
                            x = nc.vector.max(ts[:, h, 0:8], cand[:, h, :])
                        elif step == 1:
                            x = nc.vector.max_index(tp[:, h, 0:8], ts[:, h, 0:8], cand[:, h, :])
                        elif step == 2:
                            x = nc.vector.match_replace(cand2[:, h, :], ts[:, h, 0:8], cand[:, h, :], LOW)
                        elif step == 3:
                            x = nc.vector.max(ts[:, h, 8:16], cand2[:, h, :])
                        else:
                            x = nc.vector.max_index(tp[:, h, 8:16], ts[:, h, 8:16], cand2[:, h, :])
                    order(x)
                nc.vector.tensor_single_scalar(tu[:], tp[:], 4, ALU.logical_shift_right)
                order(nc.vector.tensor_single_scalar(tp[:], tp[:], 15, ALU.bitwise_and))
                nc.vector.tensor_copy(pa[:, 0], tu[:])
                order(nc.vector.tensor_copy(pa[:, 1], tp[:]))
                for half in range(2):
                    order(nc.vector.tensor_tensor(cand[:].rearrange("p h (k y) -> p (h k) y", k=TOPK),
                                                  iota[:].unsqueeze(1).to_broadcast([P, SLOTS, TOPK]),
                                                  pa[:, half].rearrange("p h k -> p (h k)").unsqueeze(2).to_broadcast([P, SLOTS, TOPK]),
                                                  ALU.is_equal))
                    order(nc.vector.tensor_tensor(cand24, cand4, ia[:, :, half, :].unsqueeze(2).to_broadcast(shape), ALU.mult))
                    order(nc.vector.tensor_reduce(ef[:, half], cand24, AX.X, ALU.add))
                nc.vector.scalar_tensor_tensor(experts[:, bass.ds(t, 1), :].rearrange("p o k -> p (o k)"),
                                               ef[:, 0].rearrange("p h k -> p (h k)"), float(NKEYS),
                                               ef[:, 1].rearrange("p h k -> p (h k)"), ALU.mult, ALU.add)
                order(nc.vector.tensor_copy(gs[:], ts[:, :, 0]))
                nc.vector.tensor_tensor(ts[:], ts[:], gs[:].unsqueeze(2).to_broadcast([P, PH, TOPK]), ALU.subtract).then_inc(shifted, 1)
                dve.wait_ge(exp_done, t + 1)
                order(nc.vector.tensor_reduce(gs[:], ts[:], AX.X, ALU.add))
                order(nc.vector.reciprocal(gs[:], gs[:]))
                g = gates[:, bass.ds(t, 1), :].rearrange("p o (h k) -> p (o h) k", h=PH)
                order(nc.vector.tensor_tensor(g, ts[:], gs[:].unsqueeze(2).to_broadcast([P, PH, TOPK]), ALU.mult))
                assert n[0] == CSTEPS, n[0]


def expert_stage(nc, a, env, tag, layer, experts, gates):
    x, h, ident = env["x"], env["h"], env["ident"]
    base = layer * MODW + 5 * D
    ROUNDS = SLOTS // RING
    with Stage(nc, tag) as s:
        ring = s.sb("ring", [P, RING, 2 * D])
        col = s.sb("col", [P, RING], I32)
        hc = s.sb("hc", [P, D])
        junk = s.sb("junk", [P, D])
        pre = s.sb("pre", [P, RING])
        wt = s.sb("wt", [P, RING])
        diag = s.sb("diag", [P, RING, P])
        zero = s.sb("zero", [P, P])
        g2 = s.sb("g2", [P, 2, D])
        py = s.ps("py", [P, D])
        g2_in, tick, slot_free, col_done, hc_done = (s.sem(n) for n in ("g2_in", "tick", "slot_free", "col_done", "hc_done"))
        row_in = [s.sem(f"row_in{i}") for i in range(RING)]
        dot_done, gelu_done, wt_done, diag_done, sum_done, gated, added, zero_done = (
            s.sem(n) for n in ("dot_done", "gelu_done", "wt_done", "diag_done", "sum_done", "gated", "added", "zero_done"))
        block = s.stack.enter_context(nc.Block())

        @block.sync
        def _(sp):
            for c in range(2):
                sp.dma_start(g2[:, c, :], broadcast_row(env["mods"][c, base:base + D])).then_inc(g2_in, 16)
            sp.wait_ge(g2_in, 32)

        @block.gpsimd
        def _(pool):
            def rounds(first, last):
                with pool.Fori(first * ROUNDS, last * ROUNDS) as i:
                    for r in range(RING):
                        n = i * RING + r
                        pool.wait_ge(slot_free, n + 1)
                        pool.sem_inc(tick, 1)
                        nc.gpsimd.tensor_copy(col[:, r:r + 1], experts[:].rearrange("p t k -> p (t k)")[:, bass.ds(n, 1)]
                                              ).then_inc(col_done, 1)
                        pool.wait_ge(col_done, n + 1)
                        pool.sem_inc(tick, 1)
                        nc.gpsimd.indirect_dma_start(ring[:, r, :], None, a[f"l{layer}_uv"],
                                                     bass.IndirectOffsetOnAxis(ap=col[:, r:r + 1], axis=0)).then_inc(row_in[r], 16)

            rounds(0, TILES)

        @block.vector
        def _(dve):
            nc.vector.memset(zero[:], 0.0).then_inc(zero_done, 1)
            dve.wait_ge(g2_in, 32)

            def tile(t, c):
                nc.vector.tensor_copy(hc[:], h[:, bass.ds(t, 1), :].rearrange("p o d -> p (o d)")).then_inc(hc_done, 1)
                dve.wait_ge(hc_done, t + 1)
                with dve.Fori(t * ROUNDS, (t + 1) * ROUNDS) as i:
                    for r in range(RING):
                        dve.wait_ge(row_in[r], i * 16 + 16)
                        dve.wait_ge(wt_done, i * RING + r + 1)
                        nc.vector.tensor_tensor_reduce(junk[:], ring[:, r, 0:D], hc[:], 1.0, 0.0, ALU.mult, ALU.add,
                                                       pre[:, r:r + 1]).then_inc(dot_done, 1)
                        dve.wait_ge(dot_done, i * RING + r + 1)
                dve.wait_ge(sum_done, t + 1)
                nc.vector.tensor_tensor(hc[:], py[:], g2[:, c, :], ALU.mult).then_inc(gated, 1)
                dve.wait_ge(gated, t + 1)
                xt = x[:, bass.ds(t, 1), :].rearrange("p o d -> p (o d)")
                nc.vector.tensor_tensor(xt, xt, hc[:], ALU.add).then_inc(added, 1)
                dve.wait_ge(added, t + 1)

            tile(0, 0)
            with dve.Fori(PROMPT_TILES, TILES) as t:
                tile(t, 1)

        @block.scalar
        def _(act):
            act.sem_inc(wt_done, RING)
            with act.Fori(0, TILES * ROUNDS) as i:
                for r in range(RING):
                    n = i * RING + r
                    act.wait_ge(dot_done, n + 1)
                    nc.scalar.activation(wt[:, r:r + 1], pre[:, r:r + 1], ACT.Gelu_apprx_tanh).then_inc(gelu_done, 1)
                    act.wait_ge(gelu_done, n + 1)
                    nc.scalar.activation(wt[:, r:r + 1], wt[:, r:r + 1], ACT.Copy,
                                         scale=gates[:].rearrange("p t k -> p (t k)")[:, bass.ds(n, 1)]).then_inc(wt_done, 1)
                    act.wait_ge(wt_done, n + RING + 1)
                    act.wait_ge(slot_free, n + 1)
                    nc.scalar.activation(diag[:, r, :], ident[:], ACT.Copy, scale=wt[:, r:r + 1]).then_inc(diag_done, 1)

        def ident_wide(c):
            return env["x0"][:, c * 512:(c + 1) * 512]

        @block.tensor
        def _(pe):
            pe.sem_inc(slot_free, RING)
            pe.wait_ge(zero_done, 1)
            with pe.Fori(0, TILES) as t:
                pe.wait_ge(gated, t) if False else None
                pe.wait_ge(hc_done, t + 1)
                for c in range(2):
                    nc.tensor.matmul(py[:, c * 512:(c + 1) * 512], zero[:], ident_wide(c), start=True, stop=False,
                                     skip_group_check=True)
                with pe.Fori(t * ROUNDS, (t + 1) * ROUNDS) as i:
                    for r in range(RING):
                        n = i * RING + r
                        pe.wait_ge(diag_done, n + 1)
                        for c in range(2):
                            mm = nc.tensor.matmul(py[:, c * 512:(c + 1) * 512], diag[:, r, :],
                                                  ring[:, r, D + c * 512:D + (c + 1) * 512], start=False, stop=False,
                                                  skip_group_check=True)
                        mm.then_inc(slot_free, 1)
                for c in range(2):
                    mm = nc.tensor.matmul(py[:, c * 512:(c + 1) * 512], zero[:], ident_wide(c), start=False, stop=True,
                                          skip_group_check=True)
                mm.then_inc(sum_done, 1)


def store_stage(nc, a, env):
    with Stage(nc, "store") as s:
        stored = s.sem("stored")
        block = s.stack.enter_context(nc.Block())

        @block.sync
        def _(sp):
            sp.dma_start(a["out_prompt"].rearrange("o p d -> p (o d)"), env["x"][:, 0, :]).then_inc(stored, 16)
            sp.dma_start(a["out_sample"].rearrange("o (t p) d -> p (o t) d", p=P), env["x"][:, 1:TILES, :]).then_inc(stored, 16)
            sp.wait_ge(stored, 32)


def peer(nc, a, env, layer, norm):
    with Stage(nc, f"peer{layer}") as s:
        experts = s.sb("experts", [P, TILES, SLOTS], I32)
        gates = s.sb("gates", [P, TILES, SLOTS])
        with Stage(nc, f"peer{layer}h") as t:
            hT = t.sb("hT", [P, DK, TOK])
            norm_stage(nc, a, env, f"pnorm{layer}", layer, norm, 1, hT)
            select_stage(nc, a, env, f"select{layer}", layer, hT, experts, gates)
        expert_stage(nc, a, env, f"expert{layer}", layer, experts, gates)


def program(nc, a):
    mods = nc.dram_tensor("mods", (2, 2 * MODW), F32).ap()
    modulation_stage(nc, a, mods)
    with Stage(nc, "core") as core:
        env = {"x": core.sb("x", [P, TILES, D]), "h": core.sb("h", [P, TILES, D]), "ident": core.sb("ident", [P, P]),
               "mods": mods}
        env["x0"] = env["x"][:, 1, :]
        load_stage(nc, a, env)
        with Stage(nc, "mix") as m:
            pr = m.sb("pr", [P, TILES, IN0])
            with Stage(nc, "mixh") as t:
                hT = t.sb("hT", [P, DK, TOK])
                norm_stage(nc, a, env, "norm0", 0, a["l0_norm1"], 0, hT)
                projection_stage(nc, "in0", hT, a["l0_w_in"], IN0, IN0 // 5, pr)
            with Stage(nc, "mixg") as t:
                la = t.sb("la", [P, TILES, 2 * QK])
                st = t.sb("st", [P, 2, LATENT_TILES, 2, DV])
                wk = t.sb("wk", [P, 2, P])
                decay_stage(nc, a, env, pr, la, st, wk)
                gla_stage(nc, a, env, pr, la, st, env["h"])
            pool_stage(nc, a, pr, env["h"])
        output_stage(nc, env, "out0", 0, env["h"], a["l0_w_out"])
        peer(nc, a, env, 0, a["l0_norm2"])
        with Stage(nc, "att1") as m:
            pr = m.sb("pr", [P, TILES, IN1])
            with Stage(nc, "att1h") as t:
                hT = t.sb("hT", [P, DK, TOK])
                norm_stage(nc, a, env, "norm1", 1, a["l1_norm1"], 0, hT)
                projection_stage(nc, "in1", hT, a["l1_w_in"], IN1, IN1 // 3, pr)
            qT = m.sb("qT", [P, TILES, QH // 2, P])
            kT = m.sb("kT", [P, KVH, TILES + 1, P])
            vc = m.sb("vc", [P, KVH * HD])
            qk_stage(nc, a, env, pr, qT, kT, vc)
            attention_stage(nc, a, env, pr, qT, kT, vc, env["h"])
        output_stage(nc, env, "out1", 1, env["h"], a["l1_w_out"])
        peer(nc, a, env, 1, a["l1_norm2"])
        store_stage(nc, a, env)


_PLAIN = ["x_prompt", "x_sample", "state_l0_gla", "cache_l1_k", "cache_l1_v", "c", "c_ctx", "l0_w_mod", "l0_b_mod",
          "l0_norm1", "l0_w_in", "l0_w_alpha_f", "l0_b_alpha_f", "l0_w_alpha_b", "l0_b_alpha_b", "l0_gla_norm",
          "l0_pool_w", "l0_pool_scale", "l0_w_out", "l0_norm2", "l0_peer_wq", "l1_w_mod", "l1_b_mod", "l1_norm1",
          "l1_w_in", "l1_q_norm", "l1_k_norm", "l1_sink", "l1_w_out", "l1_norm2", "l1_peer_wq"]
_OUTS = {"out_prompt": (1, P, D), "out_sample": (1, LATENT_TILES * P, D), "out_state": (1, 2, HEADS0, DKH, DV),
         "out_k": (1, P, KVH, HD), "out_v": (1, P, KVH, HD)}


def host_arrays(inputs):
    arrays = {n: np.ascontiguousarray(inputs[n]) for n in _PLAIN}
    for layer in range(2):
        keys = np.asarray(inputs[f"l{layer}_peer_keys"])
        arrays[f"l{layer}_peer_keys"] = np.ascontiguousarray(keys.transpose(3, 0, 1, 2).reshape(P, 2 * PH, NKEYS))
        arrays[f"l{layer}_uv"] = np.concatenate([np.asarray(inputs[f"l{layer}_peer_u"]), np.asarray(inputs[f"l{layer}_peer_v"])], 1)
    arrays["k_level_sums"], arrays["k_key_sums"], arrays["k_level_masks"] = decay_constants()
    arrays["k_pool"] = pool_constants()
    arrays["k_rope"] = rope_constants()
    win = window_constants()
    none = np.zeros((P, 1, P), np.float32)
    arrays["k_window"] = np.ascontiguousarray(np.concatenate([win, none, win[:, 0:2], none], 1))
    arrays["k_ident"] = np.eye(P, dtype=np.float32)
    arrays["k_iota"] = np.tile(np.arange(TOPK, dtype=np.float32), (P, 1))
    return arrays


def kernel(**inputs):
    import concourse.bacc as _bacc
    from concourse.bass_utils import run_bass_kernel_spmd as _run

    nc = _bacc.Bacc("TRN2", target_bir_lowering=False, num_devices=1)
    given = host_arrays(inputs)
    arrays, a = {}, {}
    for name, v in given.items():
        arrays[f"in_{name}"] = v
        a[name] = nc.dram_tensor(f"in_{name}", v.shape, mybir.dt.from_np(v.dtype), kind="ExternalInput").ap()
    for name, shape in _OUTS.items():
        a[name] = nc.dram_tensor(name, shape, F32, kind="ExternalOutput").ap()
    program(nc, a)
    r = _run(nc, [arrays], core_ids=[0])
    return tuple(r.results[0][name] for name in _OUTS)
```

```python
from contextlib import ExitStack

import numpy as np

import concourse.bass as bass
from concourse import mybir

F32 = mybir.dt.float32
I32 = mybir.dt.int32
U32 = mybir.dt.uint32
U8 = mybir.dt.uint8
ALU = mybir.AluOpType
ACT = mybir.ActivationFunctionType
AX = mybir.AxisListType

P = 128
D = 1024
DK = D // P
PROMPT_TILES = 1
LATENT_TILES = 4
TILES = PROMPT_TILES + LATENT_TILES
TOK = TILES * P
EPS = 1e-6
HEADS0, DKH, DV = 4, 64, 128
QK = HEADS0 * DKH
VW = HEADS0 * DV
LOWRANK = 16
POOL_WINDOWS = (2, 4, 8, 16)
IN0 = 2 * QK + 2 * VW + 2 * LOWRANK + VW
Q0, K0, V0, R0, Z0, PIN0 = 0, QK, 2 * QK, 2 * QK + VW, 2 * QK + 2 * VW, 2 * QK + 2 * VW + 2 * LOWRANK
LEVELS = 7
QH, KVH, HD = 16, 4, 64
IN1 = (QH + 2 * KVH) * HD
GRID_W = 64
PH, NKEYS, TOPK = 8, 128, 16
SLOTS = PH * TOPK
RING = 8
MODW = 6 * D


def decay_constants():
    u = np.arange(P)[:, None]
    x = np.arange(P)[None, :]
    sums = np.zeros((2, LEVELS + 1, P, P), np.float32)
    masks = np.zeros((2, LEVELS, P, P), np.float32)
    for lv in range(LEVELS):
        m = P >> (lv + 1)
        mid = x // (2 * m) * 2 * m + m
        upper = (x // m) % 2 == 1
        sums[0, lv] = np.where(upper, (u >= mid) & (u <= x), (u > x) & (u < mid))
        sums[1, lv] = np.where(upper, (u >= mid) & (u < x), (u >= x) & (u < mid))
        s, t = u, x
        same = s // (2 * m) == t // (2 * m)
        masks[0, lv] = same & ((s // m) % 2 == 0) & ((t // m) % 2 == 1)
        masks[1, lv] = same & ((s // m) % 2 == 1) & ((t // m) % 2 == 0)
    sums[0, LEVELS] = u <= x
    sums[1, LEVELS] = u >= x
    key = np.stack([(u > x), (u < x)]).astype(np.float32)
    scale = np.float32(1 / 16)
    return (np.ascontiguousarray(sums.transpose(2, 0, 1, 3)) * scale,
            np.ascontiguousarray(key.transpose(1, 0, 2)) * scale,
            np.ascontiguousarray(masks.transpose(2, 0, 1, 3)))


def pool_constants():
    out = np.zeros((6, len(POOL_WINDOWS), P, P), np.float32)
    tok = np.arange(P)
    for v, (first, last) in enumerate(((1, 1), (1, 0), (0, 0), (0, 1))):
        for g, w in enumerate(POOL_WINDOWS):
            lo, hi = tok - w // 2, tok + w // 2
            if first:
                lo = np.maximum(lo, 0)
            if last:
                hi = np.minimum(hi, P)
            n = (hi - lo).astype(np.float32)
            src = np.arange(P)[:, None]
            out[v, g] = ((src >= lo) & (src < hi)) / n - (src == tok)
    for g, w in enumerate(POOL_WINDOWS):
        src = np.arange(P)[:, None]
        out[4, g] = (src - P >= tok - w // 2) / np.float32(w)
        out[5, g] = (src + P < tok + w // 2) / np.float32(w)
    return np.ascontiguousarray(out.transpose(2, 0, 1, 3))


def rope_constants():
    half = HD // 2
    inv = (1.0 / (np.float32(10000.0) ** (np.arange(0, half, 2, dtype=np.float32) / half))).astype(np.float32)
    pos = np.arange(LATENT_TILES * P)
    cos, sin = [], []
    for p in (pos // GRID_W, pos % GRID_W):
        ang = p.astype(np.float32)[:, None] * inv[None, :]
        cos += [np.cos(ang), np.cos(ang)]
        sin += [-np.sin(ang), np.sin(ang)]
    shape = (LATENT_TILES, P, HD)
    return np.ascontiguousarray(np.stack([np.concatenate(cos, -1).reshape(shape), np.concatenate(sin, -1).reshape(shape)])
                                .astype(np.float32).transpose(2, 0, 1, 3))


def window_constants():
    q, k = np.arange(P)[:, None], np.arange(P)[None, :]
    out = np.zeros((P, 3, P), np.float32)
    out[:, 0] = np.where(k >= q, 0, -1e30)
    out[:, 2] = np.where(k <= q, 0, -1e30)
    return out


ENGINES = ("sync", "scalar", "vector", "tensor")


class Core:

    def __init__(self, nc, a, block, meeting):
        self.nc, self.a, self.block, self.meeting, self.meetings = nc, a, block, meeting, 0
        self.bg = None
        self.cleared = []

    def meet(self, clear=()):
        nc = self.nc
        self.meetings += 1
        n = self.meetings
        meeting = self.meeting

        @self.block.scalar
        def _(act):
            act.drain().then_inc(meeting, 1)
            act.wait_ge(meeting, 4 * n)

        @self.block.vector
        def _(dve):
            dve.drain().then_inc(meeting, 1)
            dve.wait_ge(meeting, 4 * n)

        @self.block.tensor
        def _(pe):
            pe.drain().then_inc(meeting, 1)
            pe.wait_ge(meeting, 4 * n)

        @self.block.sync
        def _(sp):
            sp.drain().then_inc(meeting, 1)
            sp.wait_ge(meeting, 4 * n)
            for sem in clear:
                sp.sem_clear(sem)

        for sem in self.cleared:
            nc.release_semaphore(sem)
        self.cleared = list(clear)


class Stage:

    def __init__(self, core, tag, units=0, rate=None):
        self.core, self.tag, self.stack, self.sems = core, tag, ExitStack(), []
        self.units = units
        self.rate, self.on_pe = rate if rate else (0.0, None)

    def __enter__(self):
        self.stack.__enter__()
        self.base = self.core.bg.goal if self.core.bg else 0
        if self.rate:
            self.core.bg.on_pe = self.on_pe
        return self

    def __exit__(self, kind, *e):
        if kind is None and self.sems:
            if self.core.bg:
                self.core.bg.align(self.base + int(self.units * self.rate))
            self.core.meet(self.sems)
        return self.stack.__exit__(kind, *e)

    def tick(self, name, eng, unit):
        if self.core.bg and self.rate:
            self.core.bg.upto(name, eng, self.base + int(unit * self.rate))

    def sb(self, name, shape, dt=F32):
        return self.stack.enter_context(self.core.nc.sbuf_tensor(f"{self.tag}_{name}", shape, dt))

    def ps(self, name, shape):
        return self.stack.enter_context(self.core.nc.psum_tensor(f"{self.tag}_{name}", shape, F32))

    def sem(self, name):
        self.sems.append(self.core.nc.alloc_semaphore(f"{self.tag}_{name}"))
        return self.sems[-1]


class Order:

    def __init__(self, eng, sem):
        self.eng, self.sem, self.n = eng, sem, 0

    def __call__(self, ins):
        ins.then_inc(self.sem, 1)
        self.n += 1
        self.eng.wait_ge(self.sem, self.n)


def broadcast_row(row):
    return row.partition_broadcast(P)


def cond_of(tiles):
    return 0 if tiles[0] < PROMPT_TILES else 1


def modulation_stage(core, layer, tag, rate=None):
    nc, a = core.nc, core.a
    CH, WSLOTS = 512, 2
    CHUNKS = MODW // CH
    with Stage(core, tag, CHUNKS, rate) as s:
        w = s.sb("w", [P, WSLOTS, DK, CH])
        cond = s.sb("cond", [P, DK, 2])
        gate = s.sb("gate", [P, DK, 2])
        act_c = s.sb("silu", [P, DK, 2])
        m = s.sb("m", [2, 2, CH])
        ps = s.ps("ps", [P, 2, CH])
        cond_in = s.sem("cond_in")
        b_in = [s.sem(f"b_in{i}") for i in range(2)]
        w_in = [s.sem(f"w_in{i}") for i in range(WSLOTS)]
        stored = [s.sem(f"stored{i}") for i in range(2)]
        exp_done, dve_order, silu_done = s.sem("exp_done"), s.sem("dve_order"), s.sem("silu_done")
        mm_done, add_done = s.sem("mm_done"), s.sem("add_done")
        block = core.block

        @block.sync
        def _(sp):
            with nc.allow_non_contiguous_dma(reason="two vectors laid onto partitions"):
                sp.dma_start(cond[:, :, 0], a["c_ctx"].rearrange("(k p) -> p k", p=P)).then_inc(cond_in, 16)
                sp.dma_start(cond[:, :, 1], a["c"].rearrange("o (k p) -> p (o k)", p=P)).then_inc(cond_in, 16)
            wv = a[f"l{layer}_w_mod"].rearrange("(k p) n -> p k n", p=P)
            bias = a[f"l{layer}_b_mod"]
            for n in range(CHUNKS + 2):
                if n >= 2:
                    sp.wait_ge(add_done, n - 1)
                    sp.dma_start(core.env["mods"][:, layer * MODW + (n - 2) * CH:layer * MODW + (n - 1) * CH],
                                 m[:, n % 2, :]).then_inc(stored[n % 2], 16)
                if n < CHUNKS:
                    if n >= WSLOTS:
                        sp.wait_ge(mm_done, n - WSLOTS + 1)
                    sp.dma_start(w[:, n % WSLOTS], wv[:, :, n * CH:(n + 1) * CH]).then_inc(w_in[n % WSLOTS], 16)
                    if n >= 2:
                        sp.wait_ge(stored[n % 2], n // 2 * 16)
                    sp.dma_start(m[:, n % 2, :], bias[n * CH:(n + 1) * CH].partition_broadcast(2)).then_inc(b_in[n % 2], 16)
            for i in range(2):
                sp.wait_ge(stored[i], CHUNKS // 2 * 16)

        @block.scalar
        def _(act):
            act.wait_ge(cond_in, 32)
            nc.scalar.activation(gate[:], cond[:], ACT.Exp, scale=-1.0).then_inc(exp_done, 1)
            for n in range(CHUNKS):
                s.tick("scalar", act, n + 1)

        @block.vector
        def _(dve):
            order = Order(dve, dve_order)
            dve.wait_ge(exp_done, 1)
            order(nc.vector.tensor_scalar_add(gate[:], gate[:], 1.0))
            order(nc.vector.reciprocal(gate[:], gate[:]))
            nc.vector.tensor_tensor(act_c[:], cond[:], gate[:], ALU.mult).then_inc(silu_done, 1)
            for n in range(CHUNKS):
                dve.wait_ge(mm_done, n + 1)
                dve.wait_ge(b_in[n % 2], n // 2 * 16 + 16)
                nc.vector.tensor_tensor(m[:, n % 2, :], m[:, n % 2, :], ps[0:2, n % 2, :], ALU.add).then_inc(add_done, 1)
                s.tick("vector", dve, n + 1)

        @block.tensor
        def _(pe):
            pe.wait_ge(silu_done, 1)
            for n in range(CHUNKS):
                pe.wait_ge(w_in[n % WSLOTS], n // WSLOTS * 16 + 16)
                if n >= 2:
                    pe.wait_ge(add_done, n - 1)
                for k in range(DK):
                    mm = nc.tensor.matmul(ps[0:2, n % 2, :], act_c[:, k, :], w[:, n % WSLOTS, k, :],
                                          start=(k == 0), stop=(k == DK - 1))
                mm.then_inc(mm_done, 1)
                s.tick("tensor", pe, n + 1)


def load_stage(core):
    nc, a, env = core.nc, core.a, core.env
    with Stage(core, "load") as s:
        loaded = s.sem("loaded")
        block = core.block

        @block.sync
        def _(sp):
            sp.dma_start(env["x"][:, 0, :], a["x_prompt"].rearrange("o p d -> p (o d)")).then_inc(loaded, 16)
            sp.dma_start(env["x"][:, 1:TILES, :], a["x_sample"].rearrange("o (t p) d -> p (o t) d", p=P)).then_inc(loaded, 16)
            sp.dma_start(env["ident"][:], a["k_ident"]).then_inc(loaded, 16)
            sp.wait_ge(loaded, 48)


def norm_stage(core, tag, tiles, layer, norm, which, hT, rate=None):
    nc, a, env = core.nc, core.a, core.env
    x, h, ident = env["x"], env["h"], env["ident"]
    c = cond_of(tiles)
    NT = len(tiles)
    base = layer * MODW + which * 3 * D
    with Stage(core, tag, NT, rate) as s:
        gain = s.sb("gain", [P, D])
        ma = s.sb("scale", [P, D])
        mb = s.sb("shift", [P, D])
        junk = s.sb("junk", [P, D])
        ss = s.sb("ss", [P, NT])
        ps = s.ps("ps", [P, 2, D])
        mod_in, sq_done, mean_done, sqrt_done = s.sem("mod_in"), s.sem("sq_done"), s.sem("mean_done"), s.sem("sqrt_done")
        dve_order, act_order, h_done, tr_done, hT_done = (s.sem("dve_order"), s.sem("act_order"), s.sem("h_done"),
                                                          s.sem("tr_done"), s.sem("hT_done"))
        block = core.block

        @block.sync
        def _(sp):
            sp.dma_start(gain[:], broadcast_row(norm)).then_inc(mod_in, 16)
            sp.dma_start(ma[:], broadcast_row(env["mods"][c, base + D:base + 2 * D])).then_inc(mod_in, 16)
            sp.dma_start(mb[:], broadcast_row(env["mods"][c, base:base + D])).then_inc(mod_in, 16)

        @block.scalar
        def _(act):
            order = Order(act, act_order)
            for i, t in enumerate(tiles):
                sq = nc.scalar.activation(junk[:], x[:, t, :], ACT.Square, accum_out=ss[:, i:i + 1])
                if i < NT - 1:
                    order(sq)
            sq.then_inc(sq_done, 1)
            act.wait_ge(mean_done, 1)
            nc.scalar.activation(ss[:], ss[:], ACT.Sqrt).then_inc(sqrt_done, 1)
            for i in range(NT):
                act.wait_ge(tr_done, i + 1)
                nc.scalar.activation(hT[:, :, i * P:(i + 1) * P],
                                     ps[:, i % 2, :].rearrange("p (k n) -> p k n", k=DK), ACT.Copy).then_inc(hT_done, 1)
                s.tick("scalar", act, i + 1)

        @block.vector
        def _(dve):
            order = Order(dve, dve_order)
            dve.wait_ge(mod_in, 48)
            order(nc.vector.scalar_tensor_tensor(ma[:], ma[:], 1.0, gain[:], ALU.add, ALU.mult))
            dve.wait_ge(sq_done, 1)
            nc.vector.tensor_scalar(ss[:], ss[:], 1.0 / D, EPS, ALU.mult, ALU.add).then_inc(mean_done, 1)
            dve.wait_ge(sqrt_done, 1)
            order(nc.vector.reciprocal(ss[:], ss[:]))
            for i, t in enumerate(tiles):
                order(nc.vector.scalar_tensor_tensor(h[:, t, :], x[:, t, :], ss[:, i:i + 1], ma[:], ALU.mult, ALU.mult))
                nc.vector.tensor_tensor(h[:, t, :], h[:, t, :], mb[:], ALU.add).then_inc(h_done, 1)
                s.tick("vector", dve, i + 1)

        @block.tensor
        def _(pe):
            for i, t in enumerate(tiles):
                pe.wait_ge(h_done, i + 1)
                if i >= 2:
                    pe.wait_ge(hT_done, i - 1)
                for k in range(DK):
                    mm = nc.tensor.transpose(ps[:, i % 2, k * P:(k + 1) * P], h[:, t, k * P:(k + 1) * P], ident[:])
                mm.then_inc(tr_done, 1)
                s.tick("tensor", pe, i + 1)


def projection_stage(core, tag, NT, hT, w_dram, n_out, chunk, out, rate=None):
    nc = core.nc
    n_chunks = n_out // chunk
    with Stage(core, tag, n_chunks * NT, rate) as s:
        w = s.sb("w", [P, 2, DK, chunk])
        ps = s.ps("ps", [P, 4, 512])
        w_in = [s.sem(f"w_in{i}") for i in range(2)]
        mm_done, out_done = s.sem("mm_done"), s.sem("out_done")
        block = core.block
        wv = w_dram.rearrange("(k p) n -> p k n", p=P)

        @block.sync
        def _(sp):
            for n in range(n_chunks):
                if n >= 2:
                    sp.wait_ge(mm_done, (n - 1) * NT)
                sp.dma_start(w[:, n % 2], wv[:, :, n * chunk:(n + 1) * chunk]).then_inc(w_in[n % 2], 16)

        @block.tensor
        def _(pe):
            for n in range(n_chunks):
                pe.wait_ge(w_in[n % 2], n // 2 * 16 + 16)
                for t in range(NT):
                    i = n * NT + t
                    if i >= 4:
                        pe.wait_ge(out_done, i - 3)
                    for k in range(DK):
                        mm = nc.tensor.matmul(ps[:, i % 4, 0:chunk], hT[:, k, t * P:(t + 1) * P], w[:, n % 2, k, :],
                                              start=(k == 0), stop=(k == DK - 1))
                    mm.then_inc(mm_done, 1)
                    s.tick("tensor", pe, i + 1)

        @block.scalar
        def _(act):
            for n in range(n_chunks):
                for t in range(NT):
                    i = n * NT + t
                    act.wait_ge(mm_done, i + 1)
                    nc.scalar.activation(out[:, t, n * chunk:(n + 1) * chunk], ps[:, i % 4, 0:chunk],
                                         ACT.Copy).then_inc(out_done, 1)
                    s.tick("scalar", act, i + 1)

        @block.vector
        def _(dve):
            for i in range(n_chunks * NT):
                if s.rate:
                    dve.wait_ge(mm_done, i + 1)
                s.tick("vector", dve, i + 1)


def output_stage(core, tag, tiles, layer, rows, w_dram, rate=None):
    nc, env = core.nc, core.env
    x, ident = env["x"], env["ident"]
    c = cond_of(tiles)
    NT = len(tiles)
    base = layer * MODW + 2 * D
    with Stage(core, tag, 2 * NT, rate) as s:
        w = s.sb("w", [P, DK, D])
        g = s.sb("gate", [P, D])
        rT = s.sb("rT", [P, min(2, NT), DK, P])
        tmp = s.sb("tmp", [P, D])
        pt = s.ps("pt", [P, D])
        po = s.ps("po", [P, 2, D])
        w_in, g_in, tr_done, rT_done = s.sem("w_in"), s.sem("g_in"), s.sem("tr_done"), s.sem("rT_done")
        mm_done, gated, added = s.sem("mm_done"), s.sem("gated"), s.sem("added")
        block = core.block

        @block.sync
        def _(sp):
            sp.dma_start(w[:], w_dram.rearrange("(k p) n -> p k n", p=P)).then_inc(w_in, 16)
            sp.dma_start(g[:], broadcast_row(env["mods"][c, base:base + D])).then_inc(g_in, 16)

        @block.tensor
        def _(pe):
            def turn(t):
                if t:
                    pe.wait_ge(rT_done, t)
                for k in range(DK):
                    mm = nc.tensor.transpose(pt[:, k * P:(k + 1) * P], rows[:, tiles[t], k * P:(k + 1) * P], ident[:])
                mm.then_inc(tr_done, 1)

            turn(0)
            pe.wait_ge(w_in, 16)
            for t in range(NT):
                if t + 1 < NT:
                    turn(t + 1)
                pe.wait_ge(rT_done, t + 1)
                if t >= 2:
                    pe.wait_ge(gated, t - 1)
                for n in range(2):
                    for k in range(DK):
                        mm = nc.tensor.matmul(po[:, t % 2, n * 512:(n + 1) * 512], rT[:, t % 2, k, :],
                                              w[:, k, n * 512:(n + 1) * 512], start=(k == 0), stop=(k == DK - 1))
                    if n == 1:
                        mm.then_inc(mm_done, 1)
                    s.tick("tensor", pe, 2 * t + n + 1)

        @block.scalar
        def _(act):
            for t in range(NT):
                act.wait_ge(tr_done, t + 1)
                if t >= 2:
                    act.wait_ge(mm_done, t - 1)
                nc.scalar.activation(rT[:, t % 2], pt[:].rearrange("p (k n) -> p k n", k=DK),
                                     ACT.Copy).then_inc(rT_done, 1)
                s.tick("scalar", act, 2 * t + 1)
                s.tick("scalar", act, 2 * t + 2)

        @block.vector
        def _(dve):
            dve.wait_ge(g_in, 16)
            for t in range(NT):
                s.tick("vector", dve, 2 * t + 1)
                dve.wait_ge(mm_done, t + 1)
                if t:
                    dve.wait_ge(added, t)
                nc.vector.tensor_tensor(tmp[:], po[:, t % 2, :], g[:], ALU.mult).then_inc(gated, 1)
                dve.wait_ge(gated, t + 1)
                xt = x[:, tiles[t], :]
                nc.vector.tensor_tensor(xt, xt, tmp[:], ALU.add).then_inc(added, 1)
                s.tick("vector", dve, 2 * t + 2)


def decay_stage(core, tag, tiles, pr, la, st, wsum_key, rate=None):
    nc, a, env = core.nc, core.a, core.env
    NT = len(tiles)
    prompt = cond_of(tiles) == 0
    with Stage(core, tag, NT, rate) as s:
        wz = s.sb("wz", [2 * LOWRANK + 1, 2 * QK])
        zT = s.sb("zT", [2 * LOWRANK + 1, P])
        sixteenth = s.sb("sixteenth", [P, 1])
        u = s.sb("u", [P, 2 * QK])
        kx = s.sb("kx", [P, 2, QK])
        ku = s.sb("ku", [P, 2, QK])
        eb = s.sb("eb", [P, NT, 4])
        cs = s.sb("cs", [P, NT, 4, DV])
        pl, pk, pb, pc, pz = (s.ps(n, [P, 512]) for n in ("pl", "pk", "pb", "pc", "pz"))
        wz_clear, wz_in, st_in, st_out = s.sem("wz_clear"), s.sem("wz_in"), s.sem("st_in"), s.sem("st_out")
        zt_tr, zt_done, z_mm, l_done, la_done = (s.sem(n) for n in ("zt_tr", "zt_done", "z_mm", "l_done", "la_done"))
        k_mm, kx_done, ku_done, b_mm, eb_done, c_mm, c_done = (
            s.sem(n) for n in ("k_mm", "kx_done", "ku_done", "b_mm", "eb_done", "c_mm", "c_done"))
        act_order, dve_order = s.sem("act_order"), s.sem("dve_order")
        block = core.block

        @block.sync
        def _(sp):
            sp.wait_ge(wz_clear, 3)
            sp.dma_start(wz[0:LOWRANK, 0:QK], a["l0_w_alpha_f"]).then_inc(wz_in, 16)
            sp.dma_start(wz[LOWRANK:2 * LOWRANK, QK:2 * QK], a["l0_w_alpha_b"]).then_inc(wz_in, 16)
            sp.dma_start(wz[2 * LOWRANK:, 0:QK], a["l0_b_alpha_f"].unsqueeze(0)).then_inc(wz_in, 16)
            sp.dma_start(wz[2 * LOWRANK:, QK:2 * QK], a["l0_b_alpha_b"].unsqueeze(0)).then_inc(wz_in, 16)
            sp.dma_start(wsum_key[:], a["k_key_sums"]).then_inc(wz_in, 16)
            for d, first in () if prompt else ((0, 0), (1, LATENT_TILES - 1)):
                sp.dma_start(st[:, d, first], a["state_l0_gla"][0, d].rearrange("(hh hp) k v -> (hp k) hh v", hp=2)
                             ).then_inc(st_in, 16)
            if not prompt:
                return
            sp.wait_ge(c_done, 1)
            for d in range(2):
                sp.dma_start(a["out_state"][0, d].rearrange("(hh hp) k v -> (hp k) hh v", hp=2),
                             cs[:, 0, 2 * d:2 * d + 2, :]).then_inc(st_out, 16)
            sp.wait_ge(st_out, 32)

        @block.tensor
        def _(pe):
            pe.wait_ge(wz_in, 80)
            def decays(t):
                if t:
                    pe.wait_ge(zt_done, t)
                nc.tensor.transpose(pz[0:2 * LOWRANK, 0:P], pr[:, t, Z0:Z0 + 2 * LOWRANK], env["ident"][:]).then_inc(zt_tr, 1)
                pe.wait_ge(zt_done, t + 1)
                if t:
                    pe.wait_ge(la_done, t)
                nc.tensor.matmul(pl[:], zT[:], wz[:], start=True, stop=True).then_inc(z_mm, 1)

            def states(t):
                pe.wait_ge(la_done, t + 1)
                if t:
                    pe.wait_ge(kx_done, t)
                    pe.wait_ge(eb_done, t)
                for d in range(2):
                    mm = nc.tensor.matmul(pk[:, d * QK:(d + 1) * QK], wsum_key[:, d, :], la[:, t, d * QK:(d + 1) * QK],
                                          start=True, stop=True)
                mm.then_inc(k_mm, 1)
                for j in range(4):
                    mm = nc.tensor.matmul(pb[:, j:j + 1], la[:, t, j * P:(j + 1) * P], sixteenth[:], start=True, stop=True)
                mm.then_inc(b_mm, 1)

            def sums(t):
                pe.wait_ge(ku_done, t + 1)
                if t:
                    pe.wait_ge(c_done, t)
                for d in range(2):
                    for head in range(HEADS0):
                        lo = 64 * (head % 2)
                        j = 2 * d + head // 2
                        mm = nc.tensor.matmul(pc[lo:lo + 64, j * DV:(j + 1) * DV], ku[:, d, head * DKH:(head + 1) * DKH],
                                              pr[:, t, V0 + head * DV:V0 + (head + 1) * DV], start=True, stop=True)
                mm.then_inc(c_mm, 1)

            decays(0)
            for t in range(NT):
                states(t)
                if t + 1 < NT:
                    decays(t + 1)
                sums(t)
                s.tick("tensor", pe, t + 1)

        @block.scalar
        def _(act):
            order = Order(act, act_order)
            act.wait_ge(wz_clear, 3)

            def decays(t):
                act.wait_ge(zt_tr, t + 1)
                if t:
                    act.wait_ge(z_mm, t)
                nc.scalar.activation(zT[0:2 * LOWRANK, :], pz[0:2 * LOWRANK, 0:P], ACT.Copy).then_inc(zt_done, 1)
                act.wait_ge(z_mm, t + 1)
                if t:
                    act.wait_ge(la_done, t)
                order(nc.scalar.activation(u[:], pl[:], ACT.Abs))
                order(nc.scalar.activation(u[:], u[:], ACT.Exp, scale=-1.0))
                nc.scalar.activation(u[:], u[:], ACT.Ln, bias=1.0).then_inc(l_done, 1)

            decays(0)
            for t in range(NT):
                act.wait_ge(k_mm, t + 1)
                if t:
                    act.wait_ge(ku_done, t)
                nc.scalar.activation(kx[:].rearrange("p d n -> p (d n)"), pk[:], ACT.Exp).then_inc(kx_done, 1)
                act.wait_ge(b_mm, t + 1)
                nc.scalar.activation(eb[:, t, :], pb[:, 0:4], ACT.Exp).then_inc(eb_done, 1)
                if t + 1 < NT:
                    decays(t + 1)
                s.tick("scalar", act, t + 1)

        @block.vector
        def _(dve):
            order = Order(dve, dve_order)
            nc.vector.memset(wz[:], 0.0).then_inc(wz_clear, 1)
            nc.vector.memset(zT[2 * LOWRANK:, :], 1.0).then_inc(wz_clear, 1)
            nc.vector.memset(sixteenth[:], 1.0 / 16).then_inc(wz_clear, 1)

            def decays(t):
                dve.wait_ge(l_done, t + 1)
                nc.vector.scalar_tensor_tensor(la[:, t, :], pl[:], 0.0, u[:], ALU.min, ALU.subtract).then_inc(la_done, 1)

            decays(0)
            for t in range(NT):
                dve.wait_ge(kx_done, t + 1)
                if t:
                    dve.wait_ge(c_mm, t)
                k_rows = pr[:, t, K0:K0 + QK].unsqueeze(1).to_broadcast([P, 2, QK])
                nc.vector.tensor_tensor(ku[:], kx[:], k_rows, ALU.mult).then_inc(ku_done, 1)
                if t + 1 < NT:
                    decays(t + 1)
                dve.wait_ge(c_mm, t + 1)
                nc.vector.tensor_copy(cs[:, t].rearrange("p j v -> p (j v)"), pc[:]).then_inc(c_done, 1)
                s.tick("vector", dve, t + 1)
            if prompt:
                return
            dve.wait_ge(st_in, 32)
            dve.wait_ge(eb_done, NT)
            dve.wait_ge(c_done, NT)
            for i in range(LATENT_TILES - 1):
                for d, (src, dst) in enumerate(((i, i + 1), (LATENT_TILES - 1 - i, LATENT_TILES - 2 - i))):
                    for hh in range(2):
                        j = 2 * d + hh
                        order(nc.vector.scalar_tensor_tensor(st[:, d, dst, hh, :], st[:, d, src, hh, :],
                                                             eb[:, src, j:j + 1],
                                                             cs[:, src, j, :], ALU.mult, ALU.add))


def gla_stage(core, tag, tiles, pr, la, st, mix, rate=None):
    nc, a, env = core.nc, core.a, core.env
    NT = len(tiles)
    latent = cond_of(tiles) == 1
    HALVES = 2
    UN = NT * HALVES
    SL = LEVELS + 1
    BATCH = 4
    BATCHES = -(-(1 + 2 * LEVELS) // BATCH)
    SC = 1 + 2 * LEVELS
    with Stage(core, tag, UN * BATCHES, rate) as s:
        wsum = s.sb("wsum", [P, 2, SL, P])
        mask = s.sb("mask", [P, 2, LEVELS, P], U8)
        gn = s.sb("gn", [P, DV])
        qkT = s.sb("qkT", [P, 4, P])
        e = s.sb("e", [P, 2, SL, P])
        qe = s.sb("qe", [P, 2, SL, P])
        wide_mask = qe[:].rearrange("p d l n -> p (d l n)")[:, 0:2 * LEVELS * P]
        ke = e
        sc = s.sb("sc", [P, 2, P])
        sq = s.sb("sq", [P, VW])
        ss = s.sb("ss", [P, HEADS0])
        sg = s.sb("sg", [P, VW])
        pd = s.ps("pd", [P, SL * P])
        pt = pd[:, 0:4 * P].rearrange("p (j n) -> p j n", j=4)
        pscore = s.ps("pscore", [P, 2, BATCH, P])
        po = s.ps("po", [P, 2, 512])
        scores_in = (pscore, pd[:].rearrange("p (hh j n) -> p hh j n", hh=2, j=BATCH))
        po_heads = po[:].rearrange("p b (hf v) -> p hf b v", v=DV)[:, 0:2]
        const_in, tr_done, qkT_done, d_mm, e_done, qe_done, ke_done = (
            s.sem(n) for n in ("const_in", "tr_done", "qkT_done", "d_mm", "e_done", "qe_done", "ke_done"))
        score_mm, score_used, o_mm, sq_done, mean_done, sqrt_done, r_exp, mix_done = (
            s.sem(n) for n in ("score_mm", "score_used", "o_mm", "sq_done", "mean_done", "sqrt_done", "r_exp", "mix_done"))
        dve_order = s.sem("dve_order")
        block = core.block

        @block.sync
        def _(sp):
            sp.dma_start(wsum[:], a["k_level_sums"]).then_inc(const_in, 16)
            sp.dma_start(wide_mask, a["k_level_masks"].rearrange("p d l n -> p (d l n)")).then_inc(const_in, 16)
            sp.dma_start(gn[:], broadcast_row(a["l0_gla_norm"])).then_inc(const_in, 16)

        @block.tensor
        def _(pe):
            pe.wait_ge(const_in, 48)
            for n in range(UN):
                t, half = divmod(n, HALVES)
                if n:
                    pe.wait_ge(e_done, 2 * n)
                if half == 0:
                    for j in range(4):
                        mm = nc.tensor.transpose(pt[:, j, :], pr[:, t, j * P:(j + 1) * P], env["ident"][:])
                    mm.then_inc(tr_done, 1)
                    pe.wait_ge(qkT_done, t + 1)
                for d in range(2):
                    if d:
                        pe.wait_ge(e_done, 2 * n + 1)
                    for c in range(2):
                        mm = nc.tensor.matmul(pd[:, c * 512:(c + 1) * 512], la[:, t, d * QK + half * P:d * QK + (half + 1) * P],
                                              wsum[:, d].rearrange("p l n -> p (l n)")[:, c * 512:(c + 1) * 512],
                                              start=True, stop=True)
                    mm.then_inc(d_mm, 1)
                for jb in range(BATCHES):
                    batch = n * BATCHES + jb
                    if jb == 0:
                        pe.wait_ge(qe_done, 2 * n + 1)
                        pe.wait_ge(ke_done, 2 * n + 1)
                    if jb == 1:
                        pe.wait_ge(e_done, 2 * n + 2)
                    if jb == 2:
                        pe.wait_ge(qe_done, 2 * n + 2)
                        pe.wait_ge(ke_done, 2 * n + 2)
                    if jb >= 2:
                        pe.wait_ge(score_used, batch - 1)
                    for j in range(jb * BATCH, min(SC, (jb + 1) * BATCH)):
                        for hh in range(2):
                            lo = 64 * hh
                            if j == 0:
                                keys, queries = qkT[lo:lo + 64, 2 + half, :], qkT[lo:lo + 64, half, :]
                            else:
                                d, lv = divmod(j - 1, LEVELS)
                                keys, queries = ke[lo:lo + 64, d, lv, :], qe[lo:lo + 64, d, lv, :]
                            mm = nc.tensor.matmul(scores_in[jb % 2][:, hh, j % BATCH, :], keys, queries, start=True, stop=True)
                    mm.then_inc(score_mm, 1)
                    s.tick("tensor", pe, batch + 1)
                pe.wait_ge(score_used, (n + 1) * BATCHES)
                if half == 0 and t:
                    pe.wait_ge(mix_done, t)
                for hh in range(2):
                    head, lo = 2 * half + hh, 64 * hh
                    mm = nc.tensor.matmul(po[:, hh, half * DV:(half + 1) * DV], sc[:, hh, :], pr[:, t, V0 + head * DV:V0 + (head + 1) * DV],
                                          start=True, stop=not latent)
                    if latent:
                        for d in range(2):
                            mm = nc.tensor.matmul(po[:, hh, half * DV:(half + 1) * DV], qe[lo:lo + 64, d, LEVELS, :],
                                                  st[lo:lo + 64, d, t, half, :], start=False, stop=(d == 1))
                mm.then_inc(o_mm, 1)

        @block.scalar
        def _(act):
            for n in range(UN):
                t, half = divmod(n, HALVES)
                if half == 0:
                    act.wait_ge(tr_done, t + 1)
                    if t:
                        act.wait_ge(o_mm, n)
                    nc.scalar.activation(qkT[:, 0:2, :], pt[:, 0:2, :], ACT.Copy, scale=DKH ** -0.5)
                    nc.scalar.activation(qkT[:, 2:4, :], pt[:, 2:4, :], ACT.Copy).then_inc(qkT_done, 1)
                if n:
                    act.wait_ge(o_mm, n)
                for d in range(2):
                    act.wait_ge(d_mm, 2 * n + d + 1)
                    nc.scalar.activation(e[:, d].rearrange("p l n -> p (l n)"), pd[:], ACT.Exp).then_inc(e_done, 1)
                for jb in range(BATCHES):
                    s.tick("scalar", act, n * BATCHES + jb + 1)
                if half == 1:
                    act.wait_ge(o_mm, n + 1)
                    if t:
                        act.wait_ge(mix_done, t)
                    nc.scalar.activation(sq[:].rearrange("p (hf b v) -> p hf b v", hf=2, b=2), po_heads, ACT.Square).then_inc(sq_done, 1)
                    nc.scalar.activation(sg[:], pr[:, t, R0:R0 + VW], ACT.Exp, scale=-1.0).then_inc(r_exp, 1)
                    act.wait_ge(mean_done, t + 1)
                    nc.scalar.activation(ss[:], ss[:], ACT.Sqrt).then_inc(sqrt_done, 1)

        @block.vector
        def _(dve):
            order = Order(dve, dve_order)
            dve.wait_ge(const_in, 48)
            order(nc.vector.tensor_copy(mask[:].rearrange("p d l n -> p (d l n)"), wide_mask))
            for n in range(UN):
                t, half = divmod(n, HALVES)
                dve.wait_ge(qkT_done, t + 1)
                if n:
                    dve.wait_ge(o_mm, n)
                qq = qkT[:, half, :].unsqueeze(1).to_broadcast([P, SL, P])
                kk = qkT[:, 2 + half, :].unsqueeze(1).to_broadcast([P, SL, P])
                for d in range(2):
                    dve.wait_ge(e_done, 2 * n + d + 1)
                    nc.vector.tensor_tensor(qe[:, d], e[:, d], qq, ALU.mult).then_inc(qe_done, 1)
                    dve.wait_ge(qe_done, 2 * n + d + 1)
                    nc.vector.tensor_tensor(ke[:, d], e[:, d], kk, ALU.mult).then_inc(ke_done, 1)
                for j in range(SC):
                    batch = n * BATCHES + j // BATCH
                    if j % BATCH == 0:
                        dve.wait_ge(score_mm, batch + 1)
                    src = scores_in[j // BATCH % 2][:, :, j % BATCH, :]
                    if j == 0:
                        x = nc.vector.tensor_scalar(sc[:], src, 2.0, None, ALU.mult)
                    else:
                        d, lv = divmod(j - 1, LEVELS)
                        x = nc.vector.copy_predicated(sc[:], mask[:, d, lv, :].unsqueeze(1).to_broadcast([P, 2, P]), src)
                    if j % BATCH == BATCH - 1 or j == SC - 1:
                        x.then_inc(score_used, 1)
                        dve.wait_ge(score_used, batch + 1)
                        s.tick("vector", dve, batch + 1)
                    else:
                        order(x)
                if half == 1:
                    dve.wait_ge(sq_done, t + 1)
                    order(nc.vector.tensor_reduce(ss[:], sq[:].rearrange("p (h v) -> p h v", h=HEADS0), AX.X, ALU.add))
                    nc.vector.tensor_scalar(ss[:], ss[:], 1.0 / DV, EPS, ALU.mult, ALU.add).then_inc(mean_done, 1)
                    dve.wait_ge(r_exp, t + 1)
                    order(nc.vector.tensor_scalar_add(sg[:], sg[:], 1.0))
                    order(nc.vector.reciprocal(sg[:], sg[:]))
                    order(nc.vector.tensor_tensor(sg[:], sg[:], pr[:, t, R0:R0 + VW], ALU.mult))
                    sg3 = sg[:].rearrange("p (h v) -> p h v", h=HEADS0)
                    order(nc.vector.tensor_tensor(sg3, sg3, gn[:].unsqueeze(1).to_broadcast([P, HEADS0, DV]), ALU.mult))
                    dve.wait_ge(sqrt_done, t + 1)
                    order(nc.vector.reciprocal(ss[:], ss[:]))
                    rstd = ss[:].rearrange("p (hf b) -> p hf b", hf=2).unsqueeze(3).to_broadcast([P, 2, 2, DV])
                    order(nc.vector.tensor_tensor(sq[:].rearrange("p (hf b v) -> p hf b v", hf=2, b=2), po_heads, rstd, ALU.mult))
                    nc.vector.tensor_tensor(mix[:, tiles[t], 0:VW], sq[:], sg[:], ALU.mult).then_inc(mix_done, 1)


def pool_stage(core, tag, tiles, pr, mix, rate=None):
    nc, a = core.nc, core.a
    NT = len(tiles)
    G = len(POOL_WINDOWS)
    with Stage(core, tag, NT, rate) as s:
        band = s.sb("band", [P, 6, G, P])
        pw = s.sb("pw", [P, G, P])
        psc = s.sb("psc", [P, VW])
        dT = s.sb("dT", [P, 2, G, P])
        pd = s.ps("pd", [P, 2, G, P])
        py = s.ps("py", [P, 2, VW])
        const_in, d_mm, d_done, y_mm, y_done = (s.sem(n) for n in ("const_in", "d_mm", "d_done", "y_mm", "y_done"))
        block = core.block

        @block.sync
        def _(sp):
            sp.dma_start(band[:], a["k_pool"]).then_inc(const_in, 16)
            sp.dma_start(pw[:], a["l0_pool_w"].rearrange("g i o -> i g o")).then_inc(const_in, 16)
            sp.dma_start(psc[:], broadcast_row(a["l0_pool_scale"])).then_inc(const_in, 16)

        @block.tensor
        def _(pe):
            pe.wait_ge(const_in, 48)
            for t in range(NT):
                first, last = t == 0, t == NT - 1
                parts = [(t, {(True, True): 0, (True, False): 1, (False, False): 2, (False, True): 3}[first, last])]
                if not first:
                    parts.append((t - 1, 4))
                if not last:
                    parts.append((t + 1, 5))
                if t >= 2:
                    pe.wait_ge(d_done, t - 1)
                for g in range(G):
                    for i, (src, v) in enumerate(parts):
                        mm = nc.tensor.matmul(pd[:, t % 2, g, :], pr[:, src, PIN0 + g * P:PIN0 + (g + 1) * P], band[:, v, g, :],
                                              start=(i == 0), stop=(i == len(parts) - 1))
                mm.then_inc(d_mm, 1)
                pe.wait_ge(d_done, t + 1)
                if t >= 2:
                    pe.wait_ge(y_done, t - 1)
                for g in range(G):
                    mm = nc.tensor.matmul(py[:, t % 2, g * P:(g + 1) * P], dT[:, t % 2, g, :], pw[:, g, :], start=True, stop=True)
                mm.then_inc(y_mm, 1)
                s.tick("tensor", pe, t + 1)

        @block.scalar
        def _(act):
            for t in range(NT):
                act.wait_ge(d_mm, t + 1)
                if t >= 2:
                    act.wait_ge(y_mm, t - 1)
                nc.scalar.activation(dT[:, t % 2], pd[:, t % 2], ACT.Copy).then_inc(d_done, 1)
                s.tick("scalar", act, t + 1)

        @block.vector
        def _(dve):
            dve.wait_ge(const_in, 48)
            for t in range(NT):
                dve.wait_ge(y_mm, t + 1)
                nc.vector.tensor_tensor(mix[:, tiles[t], VW:], py[:, t % 2, :], psc[:], ALU.mult).then_inc(y_done, 1)
                s.tick("vector", dve, t + 1)


def qk_stage(core, tag, tiles, which, pr, qT, kT, vc, rate=None):
    nc, a, env = core.nc, core.a, core.env
    NT = len(which)
    prompt = cond_of(tiles) == 0
    cache = not prompt and which[0] == 0
    KT = NT + 1 if cache else NT
    QKH = QH + KVH
    W = QKH * HD
    with Stage(core, tag, 2 * NT, rate) as s:
        gain = s.sb("gain", [P, 2, HD])
        rope = s.sb("rope", [P, 2, LATENT_TILES, HD])
        kc = s.sb("kc", [P, KVH, HD])
        sq = s.sb("sq", [P, W])
        t2 = s.sb("t2", [P, W])
        ss = s.sb("ss", [P, QKH])
        kd = s.sb("kd", [P, KVH, 2, HD])
        pq = s.ps("pq", [P, 8, P])
        pk = s.ps("pk", [P, KVH, P])
        const_in, stored, sq_done, mean_done, sqrt_done = (s.sem(n) for n in ("const_in", "stored", "sq_done", "mean_done", "sqrt_done"))
        normed, kd_done, q_tr, k_tr, q_done, k_done, dve_order = (
            s.sem(n) for n in ("normed", "kd_done", "q_tr", "k_tr", "q_done", "k_done", "dve_order"))
        block = core.block

        @block.sync
        def _(sp):
            sp.dma_start(gain[:, 0, :], broadcast_row(a["l1_q_norm"])).then_inc(const_in, 16)
            sp.dma_start(gain[:, 1, :], broadcast_row(a["l1_k_norm"])).then_inc(const_in, 16)
            if not prompt:
                sp.dma_start(rope[:], a["k_rope"]).then_inc(const_in, 16)
            if cache:
                sp.dma_start(kc[:], a["cache_l1_k"][0]).then_inc(const_in, 16)
                sp.dma_start(vc[:], a["cache_l1_v"][0].rearrange("t k d -> t (k d)")).then_inc(const_in, 16)
            if not prompt:
                return
            sp.dma_start(a["out_v"][0].rearrange("t k d -> t (k d)"), pr[:, 0, W:]).then_inc(stored, 16)
            sp.wait_ge(normed, 1)
            sp.dma_start(a["out_k"][0].rearrange("t k d -> t (k d)"), pr[:, 0, QH * HD:W]).then_inc(stored, 16)
            sp.wait_ge(stored, 32)

        @block.scalar
        def _(act):
            for t, own in enumerate(which):
                if t:
                    act.wait_ge(normed, t)
                nc.scalar.activation(sq[:], pr[:, own, 0:W], ACT.Square).then_inc(sq_done, 1)
                act.wait_ge(mean_done, t + 1)
                nc.scalar.activation(ss[:], ss[:], ACT.Sqrt).then_inc(sqrt_done, 1)
                act.wait_ge(q_tr, t + 1)
                nc.scalar.activation(qT[:, own], pq[:], ACT.Copy, scale=HD ** -0.5).then_inc(q_done, 1)
                act.wait_ge(k_tr, t + 1)
                nc.scalar.activation(kT[:, :, own, :], pk[:], ACT.Copy).then_inc(k_done, 1)
                s.tick("scalar", act, 2 * t + 1)
                s.tick("scalar", act, 2 * t + 2)
            if cache:
                act.wait_ge(k_tr, NT + 1)
                nc.scalar.activation(kT[:, :, len(tiles), :], pk[:], ACT.Copy).then_inc(k_done, 1)

        @block.vector
        def _(dve):
            order = Order(dve, dve_order)
            dve.wait_ge(const_in, 32 if prompt else 80 if cache else 48)
            for t, lt in enumerate(which):
                qk = pr[:, lt, 0:W].rearrange("p (h d) -> p h d", d=HD)
                sq3 = sq[:].rearrange("p (h d) -> p h d", d=HD)
                t23 = t2[:].rearrange("p (h d) -> p h d", d=HD)
                dve.wait_ge(sq_done, t + 1)
                order(nc.vector.tensor_reduce(ss[:], sq3, AX.X, ALU.add))
                nc.vector.tensor_scalar(ss[:], ss[:], 1.0 / HD, EPS, ALU.mult, ALU.add).then_inc(mean_done, 1)
                dve.wait_ge(sqrt_done, t + 1)
                order(nc.vector.reciprocal(ss[:], ss[:]))
                order(nc.vector.tensor_tensor(qk, qk, ss[:].unsqueeze(2).to_broadcast([P, QKH, HD]), ALU.mult))
                order(nc.vector.tensor_tensor(qk[:, 0:QH], qk[:, 0:QH], gain[:, 0:1, :].to_broadcast([P, QH, HD]), ALU.mult))
                order(nc.vector.tensor_tensor(qk[:, QH:], qk[:, QH:], gain[:, 1:2, :].to_broadcast([P, KVH, HD]), ALU.mult))
                if not prompt:
                    for x2 in range(2):
                        def part(v, j):
                            return v.rearrange("p h (g j e) -> p h g j e", g=2, j=2)[:, :, :, j, :]
                        sin = rope[:, 1, lt:lt + 1, :].rearrange("p o (g j e) -> p o g j e", g=2, j=2)[:, :, :, x2, :]
                        order(nc.vector.tensor_tensor(part(t23, x2), part(qk, 1 - x2),
                                                      sin.to_broadcast([P, QKH, 2, HD // 4]), ALU.mult))
                    order(nc.vector.tensor_tensor(qk, qk, rope[:, 0, lt:lt + 1, :].to_broadcast([P, QKH, HD]), ALU.mult))
                    order(nc.vector.tensor_tensor(qk, qk, t23, ALU.add))
                if t:
                    dve.wait_ge(k_tr, t)
                for dup in range(2):
                    i = nc.vector.tensor_copy(kd[:, :, dup, :], qk[:, QH:])
                i.then_inc(normed, 1)
                s.tick("vector", dve, 2 * t + 1)
                s.tick("vector", dve, 2 * t + 2)
            if not cache:
                return
            dve.wait_ge(k_tr, NT)
            for dup in range(2):
                i = nc.vector.tensor_copy(kd[:, :, dup, :], kc[:])
            i.then_inc(normed, 1)

        @block.tensor
        def _(pe):
            for t in range(KT):
                pe.wait_ge(normed, t + 1)
                if t < NT:
                    if t:
                        pe.wait_ge(q_done, t)
                    for j in range(8):
                        mm = nc.tensor.transpose(pq[:, j, :], pr[:, which[t], j * P:(j + 1) * P], env["ident"][:])
                    mm.then_inc(q_tr, 1)
                if t:
                    pe.wait_ge(k_done, t)
                for j in range(KVH):
                    mm = nc.tensor.transpose(pk[:, j, :], kd[:, j].rearrange("p u d -> p (u d)"), env["ident"][:])
                mm.then_inc(k_tr, 1)
                if t < NT:
                    s.tick("tensor", pe, 2 * t + 1)
                    s.tick("tensor", pe, 2 * t + 2)


def attention_stage(core, tag, tiles, which, pr, qT, kT, vc, rows, rate=None):
    nc, a, env = core.nc, core.a, core.env
    NT = len(tiles)
    prompt = cond_of(tiles) == 0
    V1 = (QH + KVH) * HD
    UN = len(which) * QH
    CTX = NT

    def keys_of(t):
        if prompt:
            return [0], 1
        if t == 0:
            return [t, t + 1, CTX], 1
        if t == NT - 1:
            return [t - 1, t, CTX], 4
        return [t - 1, t, t + 1, CTX], 0

    with Stage(core, tag, UN, rate) as s:
        win = s.sb("win", [P, 7, P])
        sink = s.sb("sink", [P, QH])
        sc = s.sb("sc", [P, 2, 4 * P])
        pT = s.sb("pT", [P, 2, 4, P])
        mx = s.sb("mx", [P, 2])
        den = s.sb("den", [P, 2, QH])
        es = s.sb("es", [P, 2, QH])
        pscore = s.ps("pscore", [P, 2, 4 * P])
        ptr = s.ps("ptr", [P, 2, 4, P])
        po = s.ps("po", [P, QH, HD])
        const_in, s_mm, max_done, neg_done, exp_done, tr_done, pT_done, o_mm, es_done, row_done, dve_order = (
            s.sem(n) for n in ("const_in", "s_mm", "max_done", "neg_done", "exp_done", "tr_done", "pT_done", "o_mm",
                               "es_done", "row_done", "dve_order"))
        block = core.block

        @block.sync
        def _(sp):
            sp.dma_start(win[:], a["k_window"]).then_inc(const_in, 16)
            sp.dma_start(sink[:], broadcast_row(a["l1_sink"])).then_inc(const_in, 16)
            sp.wait_ge(const_in, 32)

        @block.tensor
        def _(pe):
            def scores(n):
                i, head = divmod(n, QH)
                t = which[i]
                lo, g = 64 * (head % 2), head // (QH // KVH)
                keys, _ = keys_of(t)
                if n >= 2:
                    pe.wait_ge(max_done, n - 1)
                q = qT[lo:lo + 64, t, head // 2, :]
                local = [k for k in keys if k != CTX]
                mm = nc.tensor.matmul(pscore[:, n % 2, 0:len(local) * P], q,
                                      kT[lo:lo + 64, g, local[0]:local[-1] + 1, :].rearrange("p t n -> p (t n)"),
                                      start=True, stop=True)
                if CTX in keys:
                    mm = nc.tensor.matmul(pscore[:, n % 2, len(local) * P:len(keys) * P], q, kT[lo:lo + 64, g, CTX, :],
                                          start=True, stop=True)
                mm.then_inc(s_mm, 1)

            def turn(n):
                keys, _ = keys_of(which[n // QH])
                pe.wait_ge(exp_done, n + 1)
                if n >= 2:
                    pe.wait_ge(pT_done, n - 1)
                for j in range(len(keys)):
                    mm = nc.tensor.transpose(ptr[:, n % 2, j, :], sc[:, n % 2, j * P:(j + 1) * P], env["ident"][:])
                mm.then_inc(tr_done, 1)

            def values(n):
                i, head = divmod(n, QH)
                g = head // (QH // KVH)
                keys, _ = keys_of(which[i])
                pe.wait_ge(pT_done, n + 1)
                if head == 0 and i:
                    pe.wait_ge(row_done, i)
                for j, k in enumerate(keys):
                    v = vc[:, g * HD:(g + 1) * HD] if k == CTX else pr[:, k, V1 + g * HD:V1 + (g + 1) * HD]
                    mm = nc.tensor.matmul(po[:, head, :], pT[:, n % 2, j, :], v, start=(j == 0), stop=(j == len(keys) - 1))
                mm.then_inc(o_mm, 1)

            for i in range(UN + 2):
                if i < UN:
                    scores(i)
                if 1 <= i <= UN:
                    turn(i - 1)
                if i >= 2:
                    values(i - 2)
                    s.tick("tensor", pe, i - 1)

        @block.scalar
        def _(act):
            for n in range(UN):
                t, head = divmod(n, QH)
                w = len(keys_of(which[t])[0]) * P
                act.wait_ge(neg_done, n + 1)
                if head == 0 and t >= 2:
                    act.wait_ge(row_done, t - 1)
                nc.scalar.activation(sc[:, n % 2, 0:w], sc[:, n % 2, 0:w], ACT.Exp, bias=mx[:, n % 2:n % 2 + 1],
                                     accum_out=den[:, t % 2, head:head + 1]).then_inc(exp_done, 1)
                nc.scalar.activation(es[:, t % 2, head:head + 1], sink[:, head:head + 1], ACT.Exp,
                                     bias=mx[:, n % 2:n % 2 + 1]).then_inc(es_done, 1)
                if n >= 2:
                    s.tick("scalar", act, n - 1)

        @block.vector
        def _(dve):
            order = Order(dve, dve_order)
            dve.wait_ge(const_in, 32)
            for n in range(UN + 2):
                if n < UN:
                    t, head = divmod(n, QH)
                    keys, m0 = keys_of(which[t])
                    w = len(keys) * P
                    dve.wait_ge(s_mm, n + 1)
                    if n >= 2:
                        dve.wait_ge(tr_done, n - 1)
                        dve.wait_ge(es_done, n - 1)
                    nc.vector.tensor_tensor_reduce(sc[:, n % 2, 0:w], pscore[:, n % 2, 0:w],
                                                   win[:, m0:m0 + len(keys), :].rearrange("p t n -> p (t n)"), 1.0,
                                                   sink[:, head:head + 1], ALU.add, ALU.max,
                                                   mx[:, n % 2:n % 2 + 1]).then_inc(max_done, 1)
                    dve.wait_ge(max_done, n + 1)
                    nc.vector.tensor_scalar(mx[:, n % 2:n % 2 + 1], mx[:, n % 2:n % 2 + 1], -1.0, None,
                                            ALU.mult).then_inc(neg_done, 1)
                if n >= 1 and n <= UN:
                    u = n - 1
                    keys, _ = keys_of(which[u // QH])
                    dve.wait_ge(tr_done, u + 1)
                    if u >= 2:
                        dve.wait_ge(o_mm, u - 1)
                    nc.vector.tensor_copy(pT[:, u % 2, 0:len(keys), :], ptr[:, u % 2, 0:len(keys), :]).then_inc(pT_done, 1)
                if n >= 2 and (n - 2) % QH == QH - 1:
                    t = (n - 2) // QH
                    dve.wait_ge(o_mm, (t + 1) * QH)
                    dve.wait_ge(es_done, (t + 1) * QH)
                    order(nc.vector.tensor_tensor(den[:, t % 2], den[:, t % 2], es[:, t % 2], ALU.add))
                    order(nc.vector.reciprocal(den[:, t % 2], den[:, t % 2]))
                    nc.vector.tensor_tensor(rows[:, tiles[which[t]], :].rearrange("p (h d) -> p h d", d=HD), po[:],
                                            den[:, t % 2].unsqueeze(2).to_broadcast([P, QH, HD]), ALU.mult).then_inc(row_done, 1)
                if n >= 2:
                    s.tick("vector", dve, n - 1)


def query_stage(core, tag, NT, layer, hT, qT, rate=None):
    nc, a = core.nc, core.a
    HC = 2 * PH
    SLOTS_W = 4
    tok = NT * P
    with Stage(core, tag, HC, rate) as s:
        w = s.sb("w", [P, SLOTS_W, DK, P])
        pq = s.ps("pq", [P, 2, 512])
        w_in = [s.sem(f"w_in{i}") for i in range(SLOTS_W)]
        q_mm, qT_done = s.sem("q_mm"), s.sem("qT_done")
        block = core.block
        wv = a[f"l{layer}_peer_wq"].rearrange("(k p) n -> p k n", p=P)

        @block.sync
        def _(sp):
            for n in range(HC):
                if n >= SLOTS_W:
                    sp.wait_ge(q_mm, n - SLOTS_W + 1)
                sp.dma_start(w[:, n % SLOTS_W], wv[:, :, n * P:(n + 1) * P]).then_inc(w_in[n % SLOTS_W], 16)

        @block.tensor
        def _(pe):
            for n in range(HC):
                pe.wait_ge(w_in[n % SLOTS_W], n // SLOTS_W * 16 + 16)
                if n >= 2:
                    pe.wait_ge(qT_done, n - 1)
                for k in range(DK):
                    mm = nc.tensor.matmul(pq[:, n % 2, 0:tok], w[:, n % SLOTS_W, k, :], hT[:, k, :], start=(k == 0), stop=(k == DK - 1))
                mm.then_inc(q_mm, 1)
                s.tick("tensor", pe, n + 1)

        @block.scalar
        def _(act):
            for n in range(HC):
                act.wait_ge(q_mm, n + 1)
                nc.scalar.activation(qT[:, n, :], pq[:, n % 2, 0:tok], ACT.Copy).then_inc(qT_done, 1)
                s.tick("scalar", act, n + 1)

        @block.vector
        def _(dve):
            for n in range(HC):
                if rate:
                    dve.wait_ge(q_mm, n + 1)
                s.tick("vector", dve, n + 1)


def select_stage(core, tag, tile, at, layer, qT, experts, gates, rate=None):
    nc, a = core.nc, core.a
    HC = 2 * PH
    LOW = -3.0e38
    with Stage(core, tag, 21, rate) as s:
        keys = s.sb("keys", [P, HC, NKEYS])
        rest = s.sb("rest", [P, HC, NKEYS])
        vals = s.sb("vals", [P, HC, TOPK])
        i1 = s.sb("i1", [P, HC, TOPK], U32)
        idxf = s.sb("idxf", [P, HC, TOPK])
        iota = s.sb("iota", [P, TOPK])
        cand = s.sb("cand", [P, PH, TOPK * TOPK])
        cand2 = rest[:].rearrange("p (h c) n -> p h (c n)", c=2)
        ts = s.sb("ts", [P, PH, TOPK])
        tp = s.sb("tp", [P, PH, TOPK], U32)
        tu = s.sb("tu", [P, PH, TOPK], U32)
        pa = s.sb("pa", [P, 2, PH, TOPK])
        ef = s.sb("ef", [P, 2, PH, TOPK])
        gs = s.sb("gs", [P, PH])
        pscore = s.ps("pscore", [P, HC, NKEYS])
        keys_in, s_mm, dve_order, shifted, exp_done = (s.sem(n) for n in ("keys_in", "s_mm", "dve_order", "shifted", "exp_done"))
        block = core.block

        @block.sync
        def _(sp):
            sp.dma_start(keys[:], a[f"l{layer}_peer_keys"]).then_inc(keys_in, 16)
            sp.dma_start(iota[:], a["k_iota"]).then_inc(keys_in, 16)

        @block.tensor
        def _(pe):
            pe.wait_ge(keys_in, 32)
            for n in range(HC):
                mm = nc.tensor.matmul(pscore[:, n, :], qT[:, n, at * P:(at + 1) * P], keys[:, n, :], start=True, stop=True)
            mm.then_inc(s_mm, 1)
            for u in range(21):
                s.tick("tensor", pe, u + 1)

        @block.scalar
        def _(act):
            for u in range(14):
                s.tick("scalar", act, u + 1)
            act.wait_ge(shifted, 1)
            nc.scalar.activation(ts[:], ts[:], ACT.Exp).then_inc(exp_done, 1)

        @block.vector
        def _(dve):
            order = Order(dve, dve_order)
            unit = [0]

            def tick():
                unit[0] += 1
                s.tick("vector", dve, unit[0])

            def top16(rows, count, val, idx, left):
                for step in range(5):
                    for j in range(count):
                        if step == 0:
                            x = nc.vector.max(val[:, j, 0:8], rows(j))
                        elif step == 1:
                            x = nc.vector.max_index(idx[:, j, 0:8], val[:, j, 0:8], rows(j))
                        elif step == 2:
                            x = nc.vector.match_replace(left(j), val[:, j, 0:8], rows(j), LOW)
                        elif step == 3:
                            x = nc.vector.max(val[:, j, 8:16], left(j))
                        else:
                            x = nc.vector.max_index(idx[:, j, 8:16], val[:, j, 8:16], left(j))
                    order(x)
                    tick()

            dve.wait_ge(s_mm, 1)
            top16(lambda j: pscore[:, j, :], HC, vals, i1, lambda j: rest[:, j, :])
            va = vals[:].rearrange("p (h c) k -> p h c k", c=2)
            ia = idxf[:].rearrange("p (h c) k -> p h c k", c=2)
            cand4 = cand[:].rearrange("p h (x y) -> p h x y", x=TOPK)
            cand24 = cand2.rearrange("p h (x y) -> p h x y", x=TOPK)
            shape = [P, PH, TOPK, TOPK]
            nc.vector.tensor_copy(idxf[:], i1[:])
            order(nc.vector.tensor_tensor(cand4, va[:, :, 0, :].unsqueeze(3).to_broadcast(shape),
                                          va[:, :, 1, :].unsqueeze(2).to_broadcast(shape), ALU.add))
            tick()
            top16(lambda j: cand[:, j, :], PH, ts, tp, lambda j: cand2[:, j, :])
            nc.vector.tensor_single_scalar(tu[:], tp[:], 4, ALU.logical_shift_right)
            order(nc.vector.tensor_single_scalar(tp[:], tp[:], 15, ALU.bitwise_and))
            nc.vector.tensor_copy(pa[:, 0], tu[:])
            order(nc.vector.tensor_copy(pa[:, 1], tp[:]))
            dve.wait_ge(keys_in, 32)
            order(nc.vector.tensor_copy(gs[:], ts[:, :, 0]))
            nc.vector.tensor_tensor(ts[:], ts[:], gs[:].unsqueeze(2).to_broadcast([P, PH, TOPK]), ALU.subtract).then_inc(shifted, 1)
            for half in range(2):
                order(nc.vector.tensor_tensor(cand[:].rearrange("p h (k y) -> p (h k) y", k=TOPK),
                                              iota[:].unsqueeze(1).to_broadcast([P, SLOTS, TOPK]),
                                              pa[:, half].rearrange("p h k -> p (h k)").unsqueeze(2).to_broadcast([P, SLOTS, TOPK]),
                                              ALU.is_equal))
                tick()
                order(nc.vector.tensor_tensor(cand24, cand4, ia[:, :, half, :].unsqueeze(2).to_broadcast(shape), ALU.mult))
                tick()
                order(nc.vector.tensor_reduce(ef[:, half], cand24, AX.X, ALU.add))
                tick()
            order(nc.vector.scalar_tensor_tensor(experts[:, tile, :], ef[:, 0].rearrange("p h k -> p (h k)"), float(NKEYS),
                                                 ef[:, 1].rearrange("p h k -> p (h k)"), ALU.mult, ALU.add))
            dve.wait_ge(exp_done, 1)
            order(nc.vector.tensor_reduce(gs[:], ts[:], AX.X, ALU.add))
            order(nc.vector.reciprocal(gs[:], gs[:]))
            nc.vector.tensor_tensor(gates[:, tile, :].rearrange("p (h k) -> p h k", h=PH), ts[:],
                                    gs[:].unsqueeze(2).to_broadcast([P, PH, TOPK]), ALU.mult).then_inc(core.bg.selected, 1)


def places_on_pe(count):
    return [r for r in range(RING) if r * count // RING != (r + 1) * count // RING]


class Experts:
    LOOP_PLACES = places_on_pe(5)
    LAG = {"vector": 0, "scalar": 1, "tensor": 3}
    TURN_BEHIND = 3
    ADD_BEHIND = 2

    def __init__(self, core, mem):
        nc = core.nc
        self.core, self.goal, self.limit, self.first, self.added, self.ended, self.opened = core, 0, 0, 0, 0, 0, 0
        self.done = {"vector": 0, "scalar": 0, "tensor": 0}
        self.sequence = [(layer, t) for layer in range(2) for t in range(TILES)]
        self.experts = mem.sb("experts", [P, TILES, SLOTS], I32)
        self.gates = mem.sb("gates", [P, TILES, SLOTS])
        self.ring = mem.sb("ring", [P, RING, 2 * D])
        self.col = mem.sb("col", [P, RING], I32)
        self.hc = mem.sb("hc", [P, D])
        self.yv = mem.sb("yv", [P, D])
        self.wt = mem.sb("wt", [P, RING])
        self.diag = mem.sb("diag", [P, RING, P])
        self.zero = mem.sb("zero", [P, P])
        self.g2 = mem.sb("g2", [P, D])
        self.py = mem.stack.enter_context(nc.psum_tensor("sum_rows", [P, D], F32))
        new = lambda name: nc.alloc_semaphore(f"experts_{name}")
        self.selected = new("selected")
        self.col_done, self.waited, self.hc_done, self.dot_done = new("col_done"), new("waited"), new("hc_done"), new("dot_done")
        self.cleared, self.tile_done = new("cleared"), new("tile_done")
        self.gelu_done, self.wt_done, self.diag_done = new("gelu_done"), new("wt_done"), new("diag_done")
        self.used = [new(f"used{r}") for r in range(RING)]
        self.sum_done, self.order, self.zero_done = new("sum_done"), new("order"), new("zero_done")
        self.row_in = [new(f"row_in{r}") for r in range(RING)]
        self.owners, self.on_pe, self.last_add = [], places_on_pe(4), None

    def own(self, goal):
        for n in range(len(self.owners), goal):
            self.owners.append("tensor" if n % RING in self.on_pe else "vector")

    def gather_all(self):
        core, nc = self.core, self.core.nc
        rounds = SLOTS // RING

        @core.block.gpsimd
        def _(pool):
            for q, (layer, t) in enumerate(self.sequence):
                pool.wait_ge(self.selected, q + 1)
                with pool.Fori(0, rounds) as i:
                    for r in range(RING):
                        rnd = i + q * rounds
                        pool.wait_ge(self.used[r], rnd + 1)
                        pool.sem_inc(self.waited, 1)
                        nc.gpsimd.tensor_copy(self.col[:, r:r + 1], self.experts[:, t, bass.ds(i * RING + r, 1)]).then_inc(self.col_done, 1)
                        pool.wait_ge(self.col_done, rnd * RING + r + 1)
                        pool.sem_inc(self.waited, 1)
                        nc.gpsimd.indirect_dma_start(self.ring[:, r, :], None, core.a[f"l{layer}_uv"],
                                                     bass.IndirectOffsetOnAxis(ap=self.col[:, r:r + 1], axis=0)
                                                     ).then_inc(self.row_in[r], 16)

    def dot(self, dve, rnd, r):
        nc = self.core.nc
        dve.wait_ge(self.row_in[r], rnd * 16 + 16)
        nc.vector.tensor_tensor_reduce(self.ring[:, r, 0:D], self.ring[:, r, 0:D], self.hc[:], 1.0, 0.0, ALU.mult, ALU.add,
                                       self.wt[:, r:r + 1]).then_inc(self.dot_done, 1)

    def add_row(self, dve, rnd, r, before):
        nc = self.core.nc
        dve.wait_ge(self.wt_done, rnd * RING + r + 1)
        if before:
            dve.wait_ge(self.used[before[1]], before[0] + 2)
        nc.vector.scalar_tensor_tensor(self.yv[:], self.ring[:, r, D:], self.wt[:, r:r + 1], self.yv[:], ALU.mult, ALU.add
                                       ).then_inc(self.used[r], 1)

    def add_slot(self, dve, n):
        if self.owners[n] == "vector":
            self.add_row(dve, *divmod(n, RING), self.last_add)
            self.last_add = divmod(n, RING)

    def weigh(self, act, rnd, r, layer, diagonal):
        nc = self.core.nc
        n = rnd * RING + r
        act.wait_ge(self.dot_done, n + 1)
        nc.scalar.activation(self.wt[:, r:r + 1], self.wt[:, r:r + 1], ACT.Gelu_apprx_tanh).then_inc(self.gelu_done, 1)
        act.wait_ge(self.gelu_done, n + 1)
        gate = self.gates[:].rearrange("p t k -> p (t k)")[:, bass.ds((rnd - layer * TILES * (SLOTS // RING)) * RING + r, 1)]
        nc.scalar.activation(self.wt[:, r:r + 1], self.wt[:, r:r + 1], ACT.Copy, scale=gate).then_inc(self.wt_done, 1)
        if diagonal:
            act.wait_ge(self.wt_done, n + 1)
            nc.scalar.activation(self.diag[:, r, :], self.core.env["ident"][:], ACT.Copy, scale=self.wt[:, r:r + 1]
                                 ).then_inc(self.diag_done, 1)

    def sum_rows(self, pe, r, count):
        nc = self.core.nc
        pe.wait_ge(self.diag_done, count)
        for c in range(2):
            mm = nc.tensor.matmul(self.py[:, c * 512:(c + 1) * 512], self.diag[:, r, :],
                                  self.ring[:, r, D + c * 512:D + (c + 1) * 512], start=False, stop=False, skip_group_check=True)
        mm.then_inc(self.used[r], 1)

    def take_h(self, dve, q, t):
        nc = self.core.nc
        if not isinstance(q, int) or q:
            dve.wait_ge(self.dot_done, q * SLOTS)
        nc.vector.tensor_copy(self.hc[:], self.core.env["h"][:, bass.ds(t, 1), :].rearrange("p o d -> p (o d)")).then_inc(self.hc_done, 1)
        dve.wait_ge(self.hc_done, q + 1)

    def clear_sum(self, dve, q):
        nc = self.core.nc
        if not isinstance(q, int) or q:
            dve.wait_ge(self.tile_done, q)
        nc.vector.memset(self.yv[:], 0.0).then_inc(self.cleared, 1)
        dve.wait_ge(self.cleared, q + 1)

    def open_sum(self, pe, q):
        nc = self.core.nc
        if isinstance(q, int) and q == 0:
            pe.wait_ge(self.zero_done, 1)
        else:
            pe.wait_ge(self.tile_done, q)
        for c in range(DK):
            nc.tensor.matmul(self.py[:, c * P:(c + 1) * P], self.zero[:], self.zero[:], start=(c * P % 512 == 0), stop=False,
                             skip_group_check=True)

    def close_sum(self, pe):
        nc = self.core.nc
        for c in range(DK):
            mm = nc.tensor.matmul(self.py[:, c * P:(c + 1) * P], self.zero[:], self.zero[:], start=False, stop=True,
                                  skip_group_check=True)
        mm.then_inc(self.sum_done, 1)

    def end_tile(self, dve, q, t, last_add):
        nc = self.core.nc
        x = self.core.env["x"][:, bass.ds(t, 1), :].rearrange("p o d -> p (o d)")
        dve.wait_ge(self.sum_done, q + 1)
        if last_add:
            dve.wait_ge(self.used[last_add[1]], last_add[0] + 2)
        nc.vector.tensor_tensor(self.yv[:], self.yv[:], self.py[:], ALU.add).then_inc(self.order, 1)
        dve.wait_ge(self.order, 2 * q + 1)
        nc.vector.tensor_tensor(self.yv[:], self.yv[:], self.g2[:], ALU.mult).then_inc(self.order, 1)
        dve.wait_ge(self.order, 2 * q + 2)
        nc.vector.tensor_tensor(x, x, self.yv[:], ALU.add).then_inc(self.tile_done, 1)

    def prepare(self):
        nc, block = self.core.nc, self.core.block

        @block.vector
        def _(dve):
            nc.vector.memset(self.zero[:], 0.0).then_inc(self.zero_done, 1)
            for r in range(RING):
                dve.sem_inc(self.used[r], 1)

    def load_gate(self, layer, c):
        core, nc = self.core, self.core.nc
        core.meet()
        with Stage(core, f"g2_{layer}_{c}") as s:
            g_in = s.sem("g_in")
            base = layer * MODW + 5 * D

            @core.block.sync
            def _(sp):
                sp.dma_start(self.g2[:], broadcast_row(core.env["mods"][c, base:base + D])).then_inc(g_in, 16)
                sp.wait_ge(g_in, 16)

    def engine(self, name):
        return {"vector": self.core.block.vector, "scalar": self.core.block.scalar, "tensor": self.core.block.tensor}[name]

    def allow(self, tiles):
        self.limit = tiles * SLOTS

    def turn_tile(self, dve, q):
        if self.ended < q:
            self.end_tile(dve, q - 1, self.sequence[q - 1][1], self.last_add)
            self.ended = q
        self.last_add = None
        self.clear_sum(dve, q)
        self.opened = q + 1

    def add_up_to(self, dve, goal):
        for n in range(self.added, goal):
            self.add_slot(dve, n)
        self.added = max(self.added, goal)

    def step(self, name, eng, n):
        rnd, r = divmod(n, RING)
        q, at = divmod(n, SLOTS)
        layer, t = self.sequence[q]
        if name == "vector":
            if at == 0:
                self.take_h(eng, q, t)
            self.dot(eng, rnd, r)
            if at == self.TURN_BEHIND:
                self.turn_tile(eng, q)
            self.add_up_to(eng, max(q * SLOTS, n - 1) if at >= self.TURN_BEHIND else min(q * SLOTS, n - 1))
        elif name == "scalar":
            self.weigh(eng, rnd, r, layer, self.owners[n] == "tensor")
        else:
            if at == 0:
                self.open_sum(eng, q)
            if self.owners[n] == "tensor":
                self.sum_rows(eng, r, self.owners[:n + 1].count("tensor"))
            if at == SLOTS - 1:
                self.close_sum(eng)

    def upto(self, name, eng, goal):
        goal = min(goal, self.limit)
        self.own(goal)
        while self.done[name] < goal - self.LAG[name]:
            self.step(name, eng, self.done[name])
            self.done[name] += 1

    def align(self, goal):
        goal = min(goal, self.limit)
        if goal > self.goal:
            self.goal = goal
            for name in self.done:
                @self.engine(name)
                def _(eng):
                    self.upto(name, eng, goal)

    def finish(self, q):
        end = (q + 1) * SLOTS
        turned = end + self.TURN_BEHIND + 1
        if self.goal > end or (self.goal == end and self.limit > end):
            self.align(max(self.goal, turned))
            return
        whole = max(-(-self.goal // RING) * RING, q * SLOTS + RING)
        self.own(whole)
        before = self.owners.count("tensor")
        self.on_pe = self.LOOP_PLACES
        self.own(end)
        for name in self.done:
            @self.engine(name)
            def _(eng):
                while self.done[name] < whole:
                    self.step(name, eng, self.done[name])
                    self.done[name] += 1
                if name == "vector":
                    self.add_up_to(eng, whole)
                last_add = self.last_add
                if whole < end:
                    if name == "vector" and last_add:
                        eng.wait_ge(self.used[last_add[1]], last_add[0] + 2)
                    last_add = self.rounds(name, eng, whole // RING, end // RING, self.sequence[q][0], before, whole // RING) or last_add
                    if name == "tensor":
                        self.close_sum(eng)
                if name == "vector":
                    self.end_tile(eng, q, self.sequence[q][1], last_add)
                    self.ended, self.added, self.last_add = q + 1, end, None
            self.done[name] = end
        self.goal = end

    def rounds(self, name, eng, first, last, layer, before, at):
        mine = [r for r in range(RING) if r not in self.on_pe]
        with eng.Fori(first, last) as i:
            def add(r):
                if r in mine:
                    k = mine.index(r)
                    self.add_row(eng, i, r, (i, mine[k - 1]) if k else (i - 1, mine[-1]))

            for r in range(RING):
                if name == "vector":
                    self.dot(eng, i, r)
                    if r >= self.ADD_BEHIND:
                        add(r - self.ADD_BEHIND)
                    if r == RING - 1:
                        for late in range(RING - self.ADD_BEHIND, RING):
                            add(late)
                elif name == "scalar":
                    self.weigh(eng, i, r, layer, r in self.on_pe)
                elif r in self.on_pe:
                    self.sum_rows(eng, r, (i - at) * len(self.on_pe) + before + self.on_pe.index(r) + 1)
        return (last - 1, mine[-1]) if mine else None

    def tiles(self, first, last):
        back = first - self.sequence[first][1]
        n = SLOTS // RING
        before = self.owners.count("tensor")
        self.on_pe = self.LOOP_PLACES
        self.own(last * SLOTS)
        for name in self.done:
            @self.engine(name)
            def _(eng):
                with eng.Fori(first, last) as q:
                    if name == "vector":
                        self.take_h(eng, q, q - back)
                        self.clear_sum(eng, q)
                    if name == "tensor":
                        self.open_sum(eng, q)
                    last_add = self.rounds(name, eng, q * n, (q + 1) * n, self.sequence[first][0], before, first * n)
                    if name == "vector":
                        self.end_tile(eng, q, q - back, last_add)
                    if name == "tensor":
                        self.close_sum(eng)
            self.done[name] = last * SLOTS
        self.goal = self.limit = last * SLOTS


def layer0_mixer(core, tag, tiles, rates):
    env, a = core.env, core.a
    NT = len(tiles)
    with Stage(core, f"{tag}_mix") as m:
        pr = m.sb("pr", [P, NT, IN0])
        with Stage(core, f"{tag}_mixh") as t:
            hT = t.sb("hT", [P, DK, NT * P])
            norm_stage(core, f"{tag}_norm", tiles, 0, a["l0_norm1"], 0, hT, rates["norm"])
            projection_stage(core, f"{tag}_in", NT, hT, a["l0_w_in"], IN0, IN0 // 5, pr, rates["in"])
        with Stage(core, f"{tag}_gla") as t:
            la = t.sb("la", [P, NT, 2 * QK])
            st = t.sb("st", [P, 2, NT, 2, DV])
            with Stage(core, f"{tag}_wk") as u:
                wk = u.sb("wk", [P, 2, P])
                decay_stage(core, f"{tag}_decay", tiles, pr, la, st, wk, rates["decay"])
            gla_stage(core, f"{tag}_gla", tiles, pr, la, st, env["h"], rates["gla"])
        pool_stage(core, f"{tag}_pool", tiles, pr, env["h"], rates["pool"])


def layer1_rows(core, tag, tiles, pr, rates):
    a = core.a
    NT = len(tiles)
    with Stage(core, f"{tag}_atth") as t:
        hT = t.sb("hT", [P, DK, NT * P])
        norm_stage(core, f"{tag}_norm", tiles, 1, a["l1_norm1"], 0, hT, rates["norm"])
        projection_stage(core, f"{tag}_in", NT, hT, a["l1_w_in"], IN1, IN1 // 4, pr, rates["in"])


def turned_queries(pr):
    return pr[:, :, 0:QH * HD].rearrange("p t (j n) -> p t j n", j=QH // 2)


def queries(core, tag, tiles, layer, qT, rates):
    a = core.a
    NT = len(tiles)
    with Stage(core, f"{tag}_h") as t:
        hT = t.sb("hT", [P, DK, NT * P])
        norm_stage(core, f"{tag}_pnorm", tiles, layer, a[f"l{layer}_norm2"], 1, hT, rates["norm"])
        query_stage(core, f"{tag}_query", NT, layer, hT, qT, rates["query"])


def first_experts(core, tag, tile, layer, rates):
    bg = core.bg
    output_stage(core, f"{tag}_out", [tile], layer, core.env["h"], core.a[f"l{layer}_w_out"], rates["out"])
    with Stage(core, f"{tag}q") as q:
        qT = q.sb("qT", [P, 2 * PH, P])
        queries(core, tag, [tile], layer, qT, rates)
        select_stage(core, f"{tag}_select", tile, 0, layer, qT, bg.experts, bg.gates, rates["select"])


def other_experts(core, tag, tiles, layer, q0, rates):
    bg = core.bg
    bg.allow(q0 + 1)
    output_stage(core, f"{tag}_out", tiles, layer, core.env["h"], core.a[f"l{layer}_w_out"], rates["out"])
    with Stage(core, f"{tag}q") as q:
        qT = q.sb("qT", [P, 2 * PH, len(tiles) * P])
        queries(core, tag, tiles, layer, qT, rates)
        for i, t in enumerate(tiles):
            select_stage(core, f"{tag}_select{t}", t, i, layer, qT, bg.experts, bg.gates, rates["select" if i else "first select"])
            bg.allow(q0 + 2 + i)


NO_ROWS = dict.fromkeys(("norm", "in", "decay", "gla", "pool", "out", "query", "select", "qk", "attend"))
PE_0, PE_2, PE_4, PE_6, PE_8 = (places_on_pe(n) for n in (0, 2, 4, 6, 8))
PROMPT_RATES = {"norm": (7.0, PE_4), "in": (3.0, PE_2), "qk": (7.5, PE_4), "attend": (2.0, PE_2), "out": (6.0, PE_2),
                "query": (1.3, PE_0), "select": (1.7, PE_8)}
MIXER_RATES = {"norm": (2.0, PE_4), "in": (1.6, PE_0), "decay": (4.0, PE_4), "gla": (1.6, PE_8), "pool": (2.0, PE_2),
               "out": (2.0, PE_0), "query": (0.8, PE_0), "select": (1.5, PE_8)}
LATENT_RATES = {"norm": (6.0, PE_4), "in": (3.0, PE_0), "qk": (5.5, PE_4), "attend": (1.6, PE_2), "out": (5.5, PE_0),
                "query": (3.0, PE_0), "first select": (1.4, PE_8), "select": (1.8, PE_8)}


def program(nc, a):
    prompt, latents = list(range(PROMPT_TILES)), list(range(PROMPT_TILES, TILES))
    first, others = latents[0], latents[1:]
    mods = nc.dram_tensor("mods", (2, 2 * MODW), F32).ap()
    with ExitStack() as outer:
        meeting = outer.enter_context(nc.semaphore("meeting"))
        core = Core(nc, a, outer.enter_context(nc.Block()), meeting)
        mem = outer.enter_context(Stage(core, "core"))
        env = core.env = {"mods": mods}
        modulation_stage(core, 0, "mod0")
        core.env.update(x=mem.sb("x", [P, TILES, D]), h=mem.sb("h", [P, TILES, D]), ident=mem.sb("ident", [P, P]))
        load_stage(core)
        bg = Experts(core, mem)
        core.bg = bg
        bg.prepare()
        bg.gather_all()

        layer0_mixer(core, "p0", prompt, NO_ROWS)
        first_experts(core, "p0", 0, 0, NO_ROWS)
        bg.load_gate(0, 0)

        bg.allow(1)
        layer0_mixer(core, "s0", latents, MIXER_RATES)
        first_experts(core, "s0a", first, 0, MIXER_RATES)
        bg.finish(0)
        bg.load_gate(0, 1)
        other_experts(core, "s0b", others, 0, 1, LATENT_RATES)
        modulation_stage(core, 1, "mod1", (4.0, PE_0))
        with Stage(core, "p1_att") as m:
            pr = m.sb("pr", [P, PROMPT_TILES, IN1])
            layer1_rows(core, "p1", prompt, pr, PROMPT_RATES)
            qT, kT, vc = turned_queries(pr), m.sb("kT", [P, KVH, PROMPT_TILES, P]), None
            qk_stage(core, "p1_qk", prompt, [0], pr, qT, kT, vc, PROMPT_RATES["qk"])
            attention_stage(core, "p1_attend", prompt, [0], pr, qT, kT, vc, env["h"], PROMPT_RATES["attend"])
        first_experts(core, "p1", 0, 1, PROMPT_RATES)
        with Stage(core, "s1_att") as m:
            pr = m.sb("pr", [P, LATENT_TILES, IN1])
            qT, kT, vc = turned_queries(pr), m.sb("kT", [P, KVH, LATENT_TILES + 1, P]), m.sb("vc", [P, KVH * HD])
            half = LATENT_TILES // 2
            bg.allow(TILES + 1)
            bg.finish(half)
            core.meet()
            layer1_rows(core, "s1a", latents[:half], pr, LATENT_RATES)
            qk_stage(core, "s1a_qk", latents, list(range(half)), pr, qT, kT, vc, LATENT_RATES["qk"])
            attention_stage(core, "s1a_attend", latents, [0], pr, qT, kT, vc, env["h"], PROMPT_RATES["attend"])
            first_experts(core, "s1a", first, 1, PROMPT_RATES)
            bg.finish(LATENT_TILES)
            bg.load_gate(1, 0)

            bg.allow(TILES + 2)
            layer1_rows(core, "s1b", latents[half:], pr[:, half:, :], LATENT_RATES)
            qk_stage(core, "s1b_qk", latents, list(range(half, LATENT_TILES)), pr, qT, kT, vc, LATENT_RATES["qk"])
            attention_stage(core, "s1b_attend", latents, list(range(1, LATENT_TILES)), pr, qT, kT, vc, env["h"],
                            LATENT_RATES["attend"])
        bg.finish(TILES)
        bg.load_gate(1, 1)
        other_experts(core, "s1b", others, 1, 6, LATENT_RATES)
        q = bg.goal // SLOTS
        bg.finish(q)
        bg.tiles(q + 1, 2 * TILES)
        core.meet()
        store_stage(core)


def store_stage(core):
    a, env = core.a, core.env
    with Stage(core, "store") as s:
        stored = s.sem("stored")

        @core.block.sync
        def _(sp):
            sp.dma_start(a["out_prompt"].rearrange("o p d -> p (o d)"), env["x"][:, 0, :]).then_inc(stored, 16)
            sp.dma_start(a["out_sample"].rearrange("o (t p) d -> p (o t) d", p=P), env["x"][:, 1:TILES, :]).then_inc(stored, 16)
            sp.wait_ge(stored, 32)


_PLAIN = ["x_prompt", "x_sample", "state_l0_gla", "cache_l1_k", "cache_l1_v", "c", "c_ctx", "l0_w_mod", "l0_b_mod",
          "l0_norm1", "l0_w_in", "l0_w_alpha_f", "l0_b_alpha_f", "l0_w_alpha_b", "l0_b_alpha_b", "l0_gla_norm",
          "l0_pool_w", "l0_pool_scale", "l0_w_out", "l0_norm2", "l0_peer_wq", "l1_w_mod", "l1_b_mod", "l1_norm1",
          "l1_w_in", "l1_q_norm", "l1_k_norm", "l1_sink", "l1_w_out", "l1_norm2", "l1_peer_wq"]
_OUTS = {"out_prompt": (1, P, D), "out_sample": (1, LATENT_TILES * P, D), "out_state": (1, 2, HEADS0, DKH, DV),
         "out_k": (1, P, KVH, HD), "out_v": (1, P, KVH, HD)}


def host_arrays(inputs):
    arrays = {n: np.ascontiguousarray(inputs[n]) for n in _PLAIN}
    for layer in range(2):
        keys = np.asarray(inputs[f"l{layer}_peer_keys"])
        arrays[f"l{layer}_peer_keys"] = np.ascontiguousarray(keys.transpose(3, 0, 1, 2).reshape(P, 2 * PH, NKEYS))
        arrays[f"l{layer}_uv"] = np.concatenate([np.asarray(inputs[f"l{layer}_peer_u"]), np.asarray(inputs[f"l{layer}_peer_v"])], 1)
    arrays["k_level_sums"], arrays["k_key_sums"], arrays["k_level_masks"] = decay_constants()
    arrays["k_pool"] = pool_constants()
    arrays["k_rope"] = rope_constants()
    win = window_constants()
    none = np.zeros((P, 1, P), np.float32)
    arrays["k_window"] = np.ascontiguousarray(np.concatenate([win, none, win[:, 0:2], none], 1))
    arrays["k_ident"] = np.eye(P, dtype=np.float32)
    arrays["k_iota"] = np.tile(np.arange(TOPK, dtype=np.float32), (P, 1))
    return arrays


def kernel(**inputs):
    import concourse.bacc as _bacc
    from concourse.bass_utils import run_bass_kernel_spmd as _run

    nc = _bacc.Bacc("TRN2", target_bir_lowering=False, num_devices=1)
    given = host_arrays(inputs)
    arrays, a = {}, {}
    for name, v in given.items():
        arrays[f"in_{name}"] = v
        a[name] = nc.dram_tensor(f"in_{name}", v.shape, mybir.dt.from_np(v.dtype), kind="ExternalInput").ap()
    for name, shape in _OUTS.items():
        a[name] = nc.dram_tensor(name, shape, F32, kind="ExternalOutput").ap()
    program(nc, a)
    r = _run(nc, [arrays], core_ids=[0])
    return tuple(r.results[0][name] for name in _OUTS)
```
